# Optimizing a Trainium2 kernel written in Bass

```python
import math
import jax, jax.numpy as jnp
from jax import lax
import numpy as np

D_MODEL = 1024
BATCH = 1
SEQ = 1024
DEPTH = 1

MIX_WIDTH = D_MODEL
GLA_WIDTH = MIX_WIDTH // 2
GLA_HEADS = 4
GLA_DV = GLA_WIDTH // GLA_HEADS
GLA_DK = GLA_DV // 2
GLA_GATE_RANK = 16
GLA_GATE_NORMALIZER = 16.0
GLA_CHUNK = 64
SB_WIDTH = MIX_WIDTH - GLA_WIDTH
SB_HEAD_DIM = 64
SB_HEADS = SB_WIDTH // SB_HEAD_DIM
SB_BLOCK = 128
MEM_LEN = 256
MEM_HEADS = 4
MEM_HEAD_DIM = D_MODEL // MEM_HEADS
D_FF = -(-8 * D_MODEL // (3 * 256)) * 256
RMS_EPS = 1e-6
GLA_QK_W = GLA_HEADS * GLA_DK
GLA_V_W = GLA_HEADS * GLA_DV
IN_SIZES = (GLA_QK_W, GLA_QK_W, GLA_V_W, GLA_V_W, GLA_GATE_RANK, SB_WIDTH, SB_WIDTH, SB_WIDTH)
D_IN = sum(IN_SIZES)

kernel_name = "hybrid_gla_stickbreaking_memxattn_swiglu"

def rms_norm(x, w):
    xf = x.astype(jnp.float32)
    y = xf * lax.rsqrt(jnp.mean(xf * xf, axis=-1, keepdims=True) + RMS_EPS)
    return (y * w.astype(jnp.float32)).astype(x.dtype)

def split_points():
    return [int(v) for v in np.cumsum(np.array(IN_SIZES))[:-1]]

def gla_chunked(q, k, v, gk):
    B, T, H, dk = q.shape
    dv = v.shape[-1]
    C = GLA_CHUNK
    N = T // C
    out_dtype = v.dtype

    def to_chunks(a):
        d = a.shape[-1]
        return a.astype(jnp.float32).reshape(B, N, C, H, d).transpose(1, 0, 3, 2, 4)

    qc, kc, vc, gc = to_chunks(q), to_chunks(k), to_chunks(v), to_chunks(gk)
    causal = jnp.tril(jnp.ones((C, C), dtype=bool))[:, :, None]

    def step(S, inp):
        qi, ki, vi, gi = inp
        b = jnp.cumsum(gi, axis=2)
        o_inter = jnp.einsum('bhcd,bhde->bhce', qi * jnp.exp(b), S)
        diff = b[:, :, :, None, :] - b[:, :, None, :, :]
        decay = jnp.where(causal, jnp.exp(jnp.where(causal, diff, 0.0)), 0.0)
        A = jnp.einsum('bhid,bhjd,bhijd->bhij', qi, ki, decay)
        o = o_inter + jnp.einsum('bhij,bhje->bhie', A, vi)
        b_last = b[:, :, -1]
        k_dec = ki * jnp.exp(b_last[:, :, None, :] - b)
        S = jnp.exp(b_last)[..., None] * S + jnp.einsum('bhcd,bhce->bhde', k_dec, vi)
        return S, o

    S0 = jnp.zeros((B, H, dk, dv), jnp.float32)
    _, o = lax.scan(step, S0, (qc, kc, vc, gc))
    return o.transpose(1, 0, 3, 2, 4).reshape(B, T, H, dv).astype(out_dtype)

def stick_breaking_attention(q, k, v):
    B, H, T, d = q.shape
    scale = 1.0 / math.sqrt(d)
    outs = []
    for i in range(T // SB_BLOCK):
        end = (i + 1) * SB_BLOCK
        q_blk = q[:, :, i * SB_BLOCK:end]
        k_blk = k[:, :, :end]
        v_blk = v[:, :, :end]
        z = jnp.einsum('bhqd,bhkd->bhqk', q_blk, k_blk).astype(jnp.float32) * scale
        t_idx = i * SB_BLOCK + jnp.arange(SB_BLOCK)[:, None]
        s_idx = jnp.arange(end)[None, :]
        strict = s_idx < t_idx
        log_beta = jax.nn.log_sigmoid(z)
        log_1m = jnp.where(strict, jax.nn.log_sigmoid(-z), 0.0)
        rev = lax.cumsum(log_1m, axis=3, reverse=True)
        log_A = log_beta + rev - log_1m
        A = jnp.where(strict, jnp.exp(log_A), 0.0)
        outs.append(jnp.einsum('bhqk,bhkd->bhqd', A, v_blk.astype(jnp.float32)).astype(v.dtype))
    return jnp.concatenate(outs, axis=2)

def parallel_mixer(h, w_in, w_gk_up, b_gk, gla_norm_w, sb_norm_w, w_out):
    B, T, _ = h.shape
    proj = h @ w_in
    q_g, k_g, v_g, g_g, gk_lr, q_s, k_s, v_s = jnp.split(proj, split_points(), axis=-1)
    q_g = q_g.reshape(B, T, GLA_HEADS, GLA_DK) * (GLA_DK ** -0.5)
    k_g = k_g.reshape(B, T, GLA_HEADS, GLA_DK)
    v_g = v_g.reshape(B, T, GLA_HEADS, GLA_DV)
    gk = (jax.nn.log_sigmoid((gk_lr @ w_gk_up + b_gk).astype(jnp.float32)) / GLA_GATE_NORMALIZER)
    gk = gk.reshape(B, T, GLA_HEADS, GLA_DK)
    o_g = gla_chunked(q_g, k_g, v_g, gk)
    o_g = rms_norm(o_g, gla_norm_w) * jax.nn.silu(g_g.reshape(B, T, GLA_HEADS, GLA_DV))
    o_g = o_g.reshape(B, T, GLA_V_W)
    def heads(a):
        return a.reshape(B, T, SB_HEADS, SB_HEAD_DIM).transpose(0, 2, 1, 3)
    o_s = stick_breaking_attention(heads(q_s), heads(k_s), heads(v_s)).transpose(0, 2, 1, 3)
    o_s = rms_norm(o_s, sb_norm_w).reshape(B, T, SB_WIDTH)
    return jnp.concatenate([o_g, o_s], axis=-1) @ w_out

def memory_cross_attention(h, mem_n, w_mq, w_mkv, mq_norm_w, mk_norm_w, w_mo):
    B, T, _ = h.shape
    M = mem_n.shape[1]
    q = rms_norm((h @ w_mq).reshape(B, T, MEM_HEADS, MEM_HEAD_DIM), mq_norm_w)
    kv = mem_n @ w_mkv
    k, v = jnp.split(kv, 2, axis=-1)
    k = rms_norm(k.reshape(B, M, MEM_HEADS, MEM_HEAD_DIM), mk_norm_w)
    v = v.reshape(B, M, MEM_HEADS, MEM_HEAD_DIM)
    s = jnp.einsum('bthd,bmhd->bhtm', q, k).astype(jnp.float32) / math.sqrt(MEM_HEAD_DIM)
    p = jax.nn.softmax(s, axis=-1).astype(v.dtype)
    o = jnp.einsum('bhtm,bmhd->bthd', p, v).reshape(B, T, D_MODEL)
    return o @ w_mo

def swiglu(h, w_gate_up, w_down):
    gate, up = jnp.split(h @ w_gate_up, 2, axis=-1)
    return (jax.nn.silu(gate) * up) @ w_down

def setup_inputs(seed: int = 0) -> dict:
    key = jax.random.key(seed)
    ks = jax.random.split(key, 24)
    f32 = jnp.float32

    def w(k, shape, fan_in):
        return jax.random.normal(k, (DEPTH,) + shape, f32) * (fan_in ** -0.5)

    def gain(k, n):
        return 1.0 + 0.01 * jax.random.normal(k, (DEPTH, n), f32)

    return {
        "x": jax.random.normal(ks[0], (BATCH, SEQ, D_MODEL), f32),
        "mem": jax.random.normal(ks[1], (BATCH, MEM_LEN, D_MODEL), f32),
        "mix_norm_w": gain(ks[2], D_MODEL),
        "w_in": w(ks[3], (D_MODEL, D_IN), D_MODEL),
        "w_gk_up": w(ks[4], (GLA_GATE_RANK, GLA_QK_W), GLA_GATE_RANK),
        "b_gk": 0.1 * jax.random.normal(ks[5], (DEPTH, GLA_QK_W), f32),
        "gla_norm_w": gain(ks[6], GLA_DV),
        "sb_norm_w": gain(ks[7], SB_HEAD_DIM),
        "w_out": w(ks[8], (MIX_WIDTH, D_MODEL), MIX_WIDTH),
        "xattn_norm_w": gain(ks[9], D_MODEL),
        "mem_norm_w": gain(ks[10], D_MODEL),
        "w_mq": w(ks[11], (D_MODEL, D_MODEL), D_MODEL),
        "w_mkv": w(ks[12], (D_MODEL, 2 * D_MODEL), D_MODEL),
        "mq_norm_w": gain(ks[13], MEM_HEAD_DIM),
        "mk_norm_w": gain(ks[14], MEM_HEAD_DIM),
        "w_mo": w(ks[15], (D_MODEL, D_MODEL), D_MODEL),
        "ffn_norm_w": gain(ks[16], D_MODEL),
        "w_gate_up": w(ks[17], (D_MODEL, 2 * D_FF), D_MODEL),
        "w_down": w(ks[18], (D_FF, D_MODEL), D_FF),
    }

def reference(x, mem, mix_norm_w, w_in, w_gk_up, b_gk, gla_norm_w, sb_norm_w, w_out,
              xattn_norm_w, mem_norm_w, w_mq, w_mkv, mq_norm_w, mk_norm_w, w_mo,
              ffn_norm_w, w_gate_up, w_down):
    for l in range(DEPTH):
        h = rms_norm(x, mix_norm_w[l])
        x = x + parallel_mixer(h, w_in[l], w_gk_up[l], b_gk[l], gla_norm_w[l], sb_norm_w[l], w_out[l])
        h = rms_norm(x, xattn_norm_w[l])
        mem_n = rms_norm(mem, mem_norm_w[l])
        x = x + memory_cross_attention(h, mem_n, w_mq[l], w_mkv[l], mq_norm_w[l], mk_norm_w[l], w_mo[l])
        h = rms_norm(x, ffn_norm_w[l])
        x = x + swiglu(h, w_gate_up[l], w_down[l])
    return x


_drawn_inputs = setup_inputs


def setup_inputs(seed=0):
    import zlib

    import numpy as np

    out = dict(_drawn_inputs(seed))
    spreads = {}
    factors = {'mix_norm_w': 4.708,
     'b_gk': 3.433,
     'gla_norm_w': 8.0,
     'sb_norm_w': 8.0,
     'xattn_norm_w': 8.0,
     'mem_norm_w': 8.0,
     'mq_norm_w': 8.0,
     'mk_norm_w': 8.0,
     'ffn_norm_w': 8.0}
    for name, (base, spread) in spreads.items():
        noise = np.random.default_rng([zlib.crc32(name.encode()), seed]).standard_normal(out[name].shape)
        drawn = base * np.exp(spread * noise) if base else spread * noise
        out[name] = __import__('jax').numpy.asarray(drawn.astype(out[name].dtype))
    for name, factor in factors.items():
        out[name] = (out[name] * factor).astype(out[name].dtype)
    return out
```

```python
from contextlib import ExitStack

import concourse.bass as bass
from concourse import mybir

ACT = mybir.ActivationFunctionType
ALU = mybir.AluOpType
AX = mybir.AxisListType
F32 = mybir.dt.float32
F32R = mybir.dt.float32r
ds = bass.ds

P = 128
SEQ = 1024
D = 1024
KT = D // P
TT = SEQ // P
HALF = 512
PW = 256
MEM = 256
DFF = 2816
EPS = 1e-6
GH, GDK, GDV = 4, 64, 128
SBK = 32
NSB = P // SBK
GCLAMP = 38.0 * 16.0
NHEADS_SB = 8
MASKED = -1.0e30
LINEAR = 40.0

COL_QG, COL_KG, COL_VG, COL_GG, COL_GK, COL_QS, COL_KS, COL_VS = 0, 256, 512, 1024, 1536, 1552, 2064, 2576

PHASES = [
    ("h1", 16, 0, 16, 0), ("qkg", 8, 8, 0, 2), ("gk", 2, 2, 0, 1), ("gkpre", 4, 4, 0, 0),
    ("gv", 32, 32, 0, 4), ("gla", 0, 0, 0, 0), ("qks", 16, 16, 0, 4), ("vs", 16, 16, 0, 2),
    ("stick", 0, 0, 0, 0), ("mix", 16, 0, 16, 0), ("wout", 32, 0, 32, 4), ("mem", 8, 0, 8, 0),
    ("memkv", 16, 16, 0, 8), ("kt", 4, 4, 0, 0), ("h2", 16, 0, 16, 0), ("q", 20, 16, 4, 4),
    ("xatt", 0, 0, 0, 0), ("wmo", 32, 0, 32, 4), ("h3", 16, 0, 16, 0), ("ffn", 0, 0, 0, 0),
]
NCH = DFF // PW


def starts():
    at, g, a, d, w = {}, 0, 0, 0, 0
    for name, ng, na, nd, nw in PHASES:
        at[name] = (g, a, d, w)
        g, a, d, w = g + ng, a + na, d + nd, w + nw
    return at


AT = starts()
FFN_G, FFN_A, FFN_D, FFN_W = AT["ffn"]


def panel_ends():
    ends = []
    for name, ng, _, _, nw in PHASES:
        for n in range(nw):
            ends.append(AT[name][0] + ng // nw * (n + 1))
    return ends


PANEL_END = panel_ends()


class Steps:

    def __init__(self, eng, sem):
        self.eng, self.sem, self.done, self.more = eng, sem, 0, 0

    def mark(self, ins):
        ins.then_inc(self.sem, 1)
        self.done += 1

    def settle(self):
        self.eng.wait_ge(self.sem, self.done + self.more)

    def enter(self, i, per, step=1):
        self.first, self.per, self.more = self.done, per, i * (per // step)

    def leave(self, iters):
        assert self.done - self.first == self.per, self.done - self.first
        self.done, self.more = self.first + self.per * iters, 0


def build(nc, x, mem, mix_norm_w, w_in, w_gk_up, b_gk, gla_norm_w, sb_norm_w, w_out,
          xattn_norm_w, mem_norm_w, w_mq, w_mkv, mq_norm_w, mk_norm_w, w_mo,
          ffn_norm_w, w_gate_up, w_down, out):
    x_t = x.rearrange("b (t p) d -> p (b t) d", p=P)
    mem_t = mem.rearrange("b (t p) d -> p (b t) d", p=P)
    out_t = out.rearrange("b (t p) d -> p (b t) d", p=P)

    def weight(w):
        return w.rearrange("l (k p) n -> p (l k) n", p=P)

    win_v, wout_v, wmq_v, wmkv_v, wmo_v, wgu_v, wdn_v = (
        weight(w) for w in (w_in, w_out, w_mq, w_mkv, w_mo, w_gate_up, w_down))

    panels = [(win_v, COL_QG), (win_v, COL_KG), (win_v, COL_GK)]
    panels += [(win_v, COL_GG), (win_v, COL_GG + PW), (win_v, COL_VG), (win_v, COL_VG + PW)]
    panels += [(win_v, c) for c in (COL_QS, COL_QS + PW, COL_KS, COL_KS + PW, COL_VS, COL_VS + PW)]
    panels += [(wout_v, PW * n) for n in range(4)]
    panels += [(wmkv_v, PW * n) for n in range(8)]
    panels += [(wmq_v, PW * n) for n in range(4)]
    panels += [(wmo_v, PW * n) for n in range(4)]
    assert len(panels) == FFN_W == len(PANEL_END)

    with ExitStack() as ctx:
        BASE = 16512

        def at(name, kb, shape, dt=F32):
            return nc.alloc_sbuf_tensor_at(name, shape, dt, offset=BASE + int(kb * 1024))

        def sem(name):
            return ctx.enter_context(nc.semaphore(name))

        raw = [at(f"raw{s}", 8 * s, [P, KT, PW]) for s in range(3)]
        whi = [at(f"whi{s}", 24 + 16 * s, [P, KT, PW], F32R) for s in range(3)]
        wlo = [at(f"wlo{s}", 32 + 16 * s, [P, KT, PW], F32R) for s in range(3)]
        LENT_RAW, LENT = 16, 56
        H = 72
        hhi = at("hhi", H, [P, KT, SEQ], F32R)
        hlo = at("hlo", H + 32, [P, KT, SEQ], F32R)
        M, X = 136, 168
        xres = at("xres", X, [P, TT, D])
        xn = at("xn", M, [P, TT, D])
        C = 200
        ident = at("ident", C, [P, P])
        tri = at("tri", C + 0.5, [P, P])
        nones = at("nones", C + 1, [P, P])
        gmask = at("gmask", C + 1.5, [P, P])
        smask = at("smask", C + 2, [P, P])
        negm = at("negm", C + 2.5, [P, P])
        wgu16 = at("wgu16", C + 3, [16, 256])
        wrows = at("wrows", C + 4, [40, P])
        wcols = at("wcols", C + 4.5, [P, 40])
        ones1 = at("ones1", C + 4.75, [P, 4])
        ssq = at("ssq", C + 4.875, [P, 32])
        rstd = at("rstd", C + 5, [P, 32])
        lnv = at("lnv", C + 5.125, [P, 32])
        mxs = at("mxs", C + 5.25, [P, 16])
        kcomb = at("kcomb", C + 5.375, [P, 2])
        ptick = at("ptick", C + 5.4375, [P, 1])
        gout = at("gout", M, [P, TT, 512])
        kx = [at(f"kx{b}", M + 16 + 4 * b, [P, 2, NSB, P]) for b in range(2)]
        bsum = at("bsum", M + 24, [P, 2, SEQ])
        vg = at("vg", X, [P, TT, 512])
        qg = at("qg", X + 16, [P, 2, SEQ])
        kg = at("kg", X + 24, [P, 2, SEQ])
        gtmp = at("gtmp", M + 16, [P, 2, SEQ])
        lrt = at("lrt", LENT, [16, SEQ])
        qx = [at(f"qx{b}", LENT + 3 * b, [P, 3, 2, P]) for b in range(2)]
        at_sb = at("at_sb", LENT + 6, [P, 2, 2, P])
        kdt = at("kdt", LENT + 8, [P, 2 * P])
        state = at("state", LENT + 9, [P, 2, P])
        decay = [at(f"decay{b}", LENT + 10 + 0.125 * b, [P, 2]) for b in range(2)]
        gsq = at("gsq", LENT + 10.5, [P, 512])
        qs = at("qs", M + 16, [P, 4, SEQ])
        ks = at("ks", X, [P, 4, SEQ])
        vs = at("vs", X + 16, [P, TT, 512])
        os_ = at("os_", LENT, [P, TT, 512])
        qcur = at("qcur", H, [P, SEQ])
        kcur = at("kcur", H + 4, [P, SEQ])
        el = [at(f"el{b}", H + 8 + 4 * b, [P, SEQ]) for b in range(3)]
        sp_ = [at(f"sp{b}", H + 20 + 4 * b, [P, SEQ]) for b in range(2)]
        later = [at(f"later{b}", H + 28 + 4 * b, [P, SEQ]) for b in range(2)]
        att = [at(f"att{b}", H + 36 + 4 * b, [P, SEQ]) for b in range(2)]
        osq = at("osq", H + 44, [P, 512])
        memx = at("memx", LENT_RAW, [P, 2, D])
        mhi = at("mhi", M + 16, [P, KT, MEM], F32R)
        mlo = at("mlo", M + 24, [P, KT, MEM], F32R)
        kraw = at("kraw", M, [P, 2, D])
        ksq = at("ksq", M + 8, [P, 8, PW])
        khat = at("khat", LENT, [P, KT, MEM])
        vmem = at("vmem", LENT + 8, [P, 2, D])
        qt = at("qt", M, [P, KT, SEQ])
        qsq = at("qsq", LENT_RAW, [P, 4, HALF])
        prob = at("prob", LENT_RAW, [P, 4, MEM])
        probt = at("probt", LENT_RAW + 4, [P, 8, P])
        fhi = at("fhi", M, [P, 2, SEQ], F32R)
        flo = at("flo", M + 8, [P, 2, SEQ], F32R)
        fgate = at("fgate", M + 16, [P, 4, HALF])
        fhid = at("fhid", M + 24, [P, 4, HALF])

        ps_all = ctx.enter_context(nc.psum_tensor("ps_all", [P, 8, HALF], F32))
        ps = [ps_all[:, b, :] for b in range(8)]

        raw_landed = [sem(f"raw_landed{s}") for s in range(3)]
        w_split = sem("w_split")
        x_landed = [sem(f"x_landed{n}") for n in range(2)]
        xr_landed = sem("xr_landed")
        small_landed = sem("small_landed")
        mem_landed = sem("mem_landed")
        out_landed = sem("out_landed")
        pe_groups, act_freed, dve_freed = sem("pe_groups"), sem("act_freed"), sem("dve_freed")
        consts_ready = sem("consts_ready")
        wcols_turned, wcols_ready = sem("wcols_turned"), sem("wcols_ready")
        rstd_ready, xn_ready, hi_ready = sem("rstd_ready"), sem("xn_ready"), sem("hi_ready")
        act_step, dve_step, pool_step = sem("act_step"), sem("dve_step"), sem("pool_step")
        g_log = sem("g_log")
        g_x, g_e, g_m, g_t, g_a, g_at = (sem(n) for n in ("g_x", "g_e", "g_m", "g_t", "g_a", "g_at"))
        g_kd, g_o, g_kv, g_s, g_r, g_out = (sem(n) for n in ("g_kd", "g_o", "g_kv", "g_s", "g_r", "g_out"))
        st_kq, st_z, st_a, st_l, st_sp = (sem(n) for n in ("st_kq", "st_z", "st_a", "st_l", "st_sp"))
        st_arg, st_att, st_av = (sem(n) for n in ("st_arg", "st_att", "st_av"))
        st_sq, st_ss, st_r, st_o = (sem(n) for n in ("st_sq", "st_ss", "st_r", "st_o"))
        kn_ready, q_copied, q_squared = sem("kn_ready"), sem("q_copied"), sem("q_squared")
        rq_ready = sem("rq_ready")
        c_s, c_nb, c_e, c_p, c_t, c_pt = (sem(n) for n in ("c_s", "c_nb", "c_e", "c_p", "c_t", "c_pt"))
        c_o, c_lo = sem("c_o"), sem("c_lo")
        f_hid, f_hi, f_lo = sem("f_hid"), sem("f_hi"), sem("f_lo")

        WC_MIX, WC_XA, WC_MEM, WC_FFN, WC_GLA, WC_SB, WC_MQ, WC_MK, WC_BGK = 0, 8, 16, 24, 32, 33, 34, 36, 38

        block = ctx.enter_context(nc.Block())

        @block.sync
        def _(sp):
            for hf in range(2):
                for t in range(4 * hf, 4 * hf + 4):
                    sp.dma_start(xres[:, t, :], x_t[:, t, :]).then_inc(x_landed[hf], 16)
                if hf == 0:
                    sp.wait_ge(consts_ready, 1)
                    rows = [(WC_MIX, mix_norm_w), (WC_XA, xattn_norm_w), (WC_MEM, mem_norm_w),
                            (WC_FFN, ffn_norm_w), (WC_GLA, gla_norm_w), (WC_MQ, mq_norm_w),
                            (WC_MK, mk_norm_w), (WC_BGK, b_gk)]
                    for r, w in rows:
                        n = w.shape[1] // P
                        sp.dma_start(wrows[r:r + n, :], w.rearrange("l (r c) -> (l r) c", c=P)).then_inc(small_landed, 16)
                    for j in range(2):
                        sp.dma_start(wrows[WC_SB:WC_SB + 1, 64 * j:64 * j + 64], sb_norm_w).then_inc(small_landed, 16)
                    sp.dma_start(wgu16[:, :], w_gk_up.rearrange("l r c -> (l r) c")).then_inc(small_landed, 16)
            for p, (view, col) in enumerate(panels):
                if p >= 2:
                    sp.wait_ge(w_split, p - 1)
                sp.dma_start(raw[p % 2][:], view[:, :, col:col + PW]).then_inc(raw_landed[p % 2], 16)
                if p == AT["wout"][3] + 1:
                    sp.wait_ge(st_o, NHEADS_SB)
                    for t in range(TT):
                        sp.dma_start(xres[:, t, :], x_t[:, t, :]).then_inc(xr_landed, 16)
                if p == AT["gv"][3]:
                    sp.dma_start(memx[:], mem_t).then_inc(mem_landed, 16)

            def load_gate(slot, c):
                sp.dma_start(raw[slot][:], wgu_v[:, :, ds(c * PW, PW)]).then_inc(raw_landed[slot], 16)

            def load_up(slot, c):
                sp.dma_start(raw[slot][:], wgu_v[:, :, ds(c * PW + DFF, PW)]).then_inc(raw_landed[slot], 16)

            def load_down(slot, c):
                dst = raw[slot][:].rearrange("p (k a) n -> p k (a n)", k=2)
                sp.dma_start(dst, wdn_v[:, ds(c * 2, 2), :]).then_inc(raw_landed[slot], 16)

            sp.wait_ge(w_split, FFN_W)
            load_gate(0, 0)
            load_up(1, 0)
            sp.wait_ge(c_lo, TT)
            with sp.Fori(0, NCH - 1) as i:
                sp.wait_ge(w_split, FFN_W + i * 3)
                load_gate(2, i + 1)
                sp.wait_ge(w_split, FFN_W + 1 + i * 3)
                load_down(0, i)
                sp.wait_ge(w_split, FFN_W + 2 + i * 3)
                load_up(1, i + 1)
            sp.wait_ge(w_split, FFN_W + 3 * (NCH - 1))
            load_down(2, NCH - 1)
            for t in range(TT):
                sp.wait_ge(dve_freed, FFN_D + (NCH - 1) * 16 + 2 * t + 2)
                sp.dma_start(out_t[:, t, :], xres[:, t, :]).then_inc(out_landed, 16)
            sp.wait_ge(out_landed, 16 * TT)

        @block.gpsimd
        def _(pool):
            st = Steps(pool, pool_step)
            for t, v in ((ident, 0.0), (tri, -1.0), (nones, -1.0), (gmask, 1.0), (smask, 1.0), (negm, MASKED), (ones1, 1.0)):
                st.mark(pool.memset(t[:], v))
            st.mark(pool.memset(wrows[:], 0.0))
            st.settle()

            def tri_select(t, op, base, mult, step, fill):
                return pool.affine_select(out=t[:], in_=t[:], compare_op=op, fill=fill, base=base,
                                          pattern=[[step, P]], channel_multiplier=mult)

            st.mark(tri_select(ident, ALU.not_equal, 0, 1, -1, 1.0))
            st.mark(tri_select(tri, ALU.is_ge, 0, 1, -1, 0.0))
            st.mark(tri_select(gmask, ALU.is_ge, 0, -1, 1, 0.0))
            st.mark(tri_select(smask, ALU.is_gt, 0, -1, 1, 0.0))
            tri_select(negm, ALU.is_ge, 0, 1, -1, 0.0).then_inc(consts_ready, 1)

            def split(slot):
                st.mark(pool.tensor_tensor(ptick[:], ones1[:, 0:1], ones1[:, 0:1], ALU.mult))
                st.mark(pool.tensor_copy(whi[slot][:], raw[slot][:]))
                st.settle()
                pool.tensor_tensor(wlo[slot][:], raw[slot][:], whi[slot][:].bitcast(F32),
                                   ALU.subtract).then_inc(w_split, 1)

            for p in range(FFN_W):
                pool.wait_ge(raw_landed[p % 2], 16 * (p // 2 + 1))
                if p >= 2:
                    pool.wait_ge(pe_groups, PANEL_END[p - 2])
                split(p % 2)
            n0, n1 = 16 * ((FFN_W + 1) // 2), 16 * (FFN_W // 2)
            pool.wait_ge(raw_landed[0], n0 + 16)
            pool.wait_ge(pe_groups, PANEL_END[FFN_W - 1])
            split(0)
            pool.wait_ge(raw_landed[1], n1 + 16)
            split(1)
            pool.wait_ge(c_lo, TT)
            with pool.Fori(0, NCH - 1) as i:
                st.enter(i, 6)
                pool.wait_ge(raw_landed[2], i * 16 + 16)
                pool.wait_ge(pe_groups, FFN_G - 12 + i * 24)
                split(2)
                pool.wait_ge(raw_landed[0], i * 16 + n0 + 32)
                pool.wait_ge(pe_groups, FFN_G + 4 + i * 24)
                split(0)
                pool.wait_ge(raw_landed[1], i * 16 + n1 + 32)
                pool.wait_ge(pe_groups, FFN_G + 8 + i * 24)
                split(1)
                st.leave(NCH - 1)
            pool.wait_ge(raw_landed[2], 16 * NCH)
            pool.wait_ge(pe_groups, FFN_G + 8 + (NCH - 2) * 24 + 4)
            split(2)

        @block.tensor
        def _(pe):
            def phase(name):
                _, a, d, _ = AT[name]
                if a:
                    pe.wait_ge(act_freed, a)
                if d:
                    pe.wait_ge(dve_freed, d)

            def prep(name, src, xn_base):
                d0 = AT[name][2]
                for hf in range(2):
                    if xn_base is not None:
                        pe.wait_ge(xn_ready, xn_base + 4 * hf + 4)
                    for k in range(KT):
                        g = hf * KT + k
                        if g >= 8:
                            pe.wait_ge(dve_freed, d0 + g - 7)
                        for n in range(4):
                            ins = pe.transpose(ps[g % 8][:, n * P:(n + 1) * P], src(4 * hf + n, k), ident[:])
                        ins.then_inc(pe_groups, 1)

            def three(dst, s_hi, s_lo, m_hi, m_lo, first, last):
                pe.matmul(dst, s_hi, m_hi, start=first, stop=False)
                pe.matmul(dst, s_lo, m_hi, start=False, stop=False)
                return pe.matmul(dst, s_hi, m_lo, start=False, stop=last)

            def feature_panel(slot, bank0, tiles=2, wait_free=None):
                for j in range(tiles):
                    for hf in range(2):
                        g = 2 * j + hf
                        if wait_free is not None:
                            wait_free(g)
                        c = slice(hf * HALF, (hf + 1) * HALF)
                        for k in range(KT):
                            ins = three(ps[bank0 + g], whi[slot][:, k, j * P:(j + 1) * P], wlo[slot][:, k, j * P:(j + 1) * P],
                                        hhi[:, k, c], hlo[:, k, c], k == 0, k == KT - 1)
                        ins.then_inc(pe_groups, 1)

            def token_panel(slot, bank0, a_hi, a_lo, tiles, wait_free=None):
                for t in range(tiles):
                    if wait_free is not None:
                        wait_free(t)
                    for k in range(KT):
                        ins = three(ps[bank0 + t][:, 0:PW], a_hi[:, k, t * P:(t + 1) * P], a_lo[:, k, t * P:(t + 1) * P],
                                    whi[slot][:, k, :], wlo[slot][:, k, :], k == 0, k == KT - 1)
                    ins.then_inc(pe_groups, 1)

            def feature_phase(name):
                _, a0, _, w0 = AT[name]
                n = [nw for nm, _, _, _, nw in PHASES if nm == name][0]
                phase(name)
                with pe.Fori(0, n // 2) as i:
                    for j in range(2):
                        pe.wait_ge(w_split, i * 2 + w0 + j + 1)
                        feature_panel((w0 + j) % 2, 4 * j, wait_free=lambda g: pe.wait_ge(act_freed, i * 8 + a0 + 4 * j + g - 7))

            def token_phase(name, freed, f0):
                w0 = AT[name][3]
                n = [nw for nm, _, _, _, nw in PHASES if nm == name][0]
                phase(name)
                with pe.Fori(0, n // 2) as i:
                    for j in range(2):
                        pe.wait_ge(w_split, i * 2 + w0 + j + 1)
                        token_panel((w0 + j) % 2, 0, hhi, hlo, TT,
                                    wait_free=lambda t: pe.wait_ge(freed, i * 16 + f0 + 8 * j + t - 7))

            pe.wait_ge(consts_ready, 1)
            pe.wait_ge(small_landed, 16 * 11)
            pe.transpose(ps[7][:, 0:40], wrows[:], ident[0:40, 0:40]).then_inc(wcols_turned, 1)

            prep("h1", lambda t, k: xres[:, t, k * P:(k + 1) * P], 0)

            phase("qkg")
            for j in range(2):
                pe.wait_ge(w_split, j + 1)
                feature_panel(j, 4 * j)
            phase("gk")
            pe.wait_ge(w_split, 3)
            feature_panel(0, 0, tiles=1)
            phase("gkpre")
            for pr in range(2):
                for hf in range(2):
                    pe.matmul(ps[2 * pr + hf], wgu16[:, pr * P:(pr + 1) * P], lrt[:, hf * HALF:(hf + 1) * HALF],
                              start=True, stop=True).then_inc(pe_groups, 1)
            token_phase("gv", act_freed, AT["gv"][1])

            phase("gla")

            def gla_scores(c, b):
                pe.wait_ge(g_m, c + 1)
                for pr in range(2):
                    ins = pe.transpose(ps[2][:, pr * P:(pr + 1) * P], qx[b][:, 2, pr, :], ident[:])
                ins.then_inc(g_t, 1)
                for pr in range(2):
                    for r in range(2):
                        rows = slice(64 * r, 64 * r + 64)
                        for s in range(NSB):
                            ins = pe.matmul(ps[r][:, pr * P + s * SBK:pr * P + (s + 1) * SBK], kx[b][rows, pr, s, :],
                                            qx[b][rows, 0, pr, s * SBK:(s + 1) * SBK], start=True, stop=True)
                ins.then_inc(g_a, 1)

            def gla_outputs(c, b):
                pe.wait_ge(g_at, c + 1)
                pe.wait_ge(g_s, c + 1)
                for h in range(GH):
                    pr, r = h // 2, h % 2
                    dst = ps[5 + r][:, pr * GDV:(pr + 1) * GDV]
                    pe.matmul(dst, at_sb[:, r, pr, :], vg[:, ds(c, 1), h * GDV:(h + 1) * GDV],
                              start=(pr == 0), stop=False, skip_group_check=True)
                    rows = slice(64 * r, 64 * r + 64)
                    ins = pe.matmul(dst, qx[b][rows, 1, pr, :], state[rows, pr, :],
                                    start=False, stop=True, skip_group_check=True)
                ins.then_inc(g_o, 1)
                pe.wait_ge(g_kd, c + 1)
                for pr in range(2):
                    ins = pe.matmul(ps[3 + pr][:, 0:2 * GDV], kdt[:, pr * P:(pr + 1) * P],
                                    vg[:, ds(c, 1), pr * 2 * GDV:(pr + 1) * 2 * GDV], start=True, stop=True)
                ins.then_inc(g_kv, 1)

            def gla_turn(c, b, more):
                gla_outputs(c, b)
                if more:
                    gla_scores(c + 1, 1 - b)

            gla_scores(0, 0)
            with pe.Fori(0, TT - 2, 2) as c:
                gla_turn(c, 0, True)
                gla_turn(c + 1, 1, True)
            gla_turn(TT - 2, 0, True)
            gla_turn(TT - 1, 1, False)

            pe.wait_ge(g_out, TT)
            feature_phase("qks")
            token_phase("vs", act_freed, AT["vs"][1])

            phase("stick")
            zb = [ps_all[:, 2 * b:2 * b + 2, :].rearrange("p b c -> p (b c)") for b in range(3)]

            def pieces(c0):
                return [(c0, HALF), (HALF, SEQ)] if c0 < HALF else [(c0, SEQ)]

            with pe.Fori(0, 4) as i:
                def scores(m):
                    r, s = m // 8, 7 - m % 8
                    if m >= 3:
                        pe.wait_ge(st_att, i * 16 + m - 2)
                    rows = slice(64 * r, 64 * r + 64)
                    for a, b in pieces(s * P):
                        ins = pe.matmul(zb[m % 3][:, a:b], kcur[rows, s * P:(s + 1) * P], qcur[rows, a:b],
                                        start=True, stop=False, skip_group_check=True)
                    ins.then_inc(st_z, 1)

                def exponent(m):
                    s = 7 - m % 8
                    pe.wait_ge(st_sp, i * 16 + m + 1)
                    z = zb[m % 3]
                    pe.matmul(z[:, s * P:(s + 1) * P], ident[:], negm[:], start=False, stop=False, skip_group_check=True)
                    if s < 7:
                        for a, b in pieces((s + 1) * P):
                            pe.matmul(z[:, a:b], nones[:], later[(m - 1) % 2][:, a:b],
                                      start=False, stop=False, skip_group_check=True)
                    for a, b in pieces(s * P):
                        ins = pe.matmul(z[:, a:b], tri[:], sp_[m % 2][:, a:b], start=False, stop=True, skip_group_check=True)
                    ins.then_inc(st_arg, 1)

                def values(m):
                    r, s = m // 8, 7 - m % 8
                    pe.wait_ge(st_att, i * 16 + m + 1)
                    for t in range(s, TT):
                        ins = pe.matmul(ps[6 + r][:, t * 64:(t + 1) * 64], att[m % 2][:, t * P:(t + 1) * P],
                                        vs[:, s, ds(i * P + 64 * r, 64)],
                                        start=(s == 7), stop=(s == 0), skip_group_check=True)
                    ins.then_inc(st_av, 1)

                pe.wait_ge(st_kq, i + 1)
                scores(0)
                scores(1)
                for m in range(16):
                    exponent(m)
                    if m < 14:
                        scores(m + 2)
                    if m >= 1:
                        values(m - 1)
                values(15)

            pe.wait_ge(st_o, NHEADS_SB)
            phase("mix")
            prep("mix", lambda t, k: gout[:, t, k * P:(k + 1) * P] if k < 4 else os_[:, t, (k - 4) * P:(k - 3) * P], None)
            token_phase("wout", dve_freed, AT["wout"][2])

            phase("mem")
            pe.wait_ge(xn_ready, 9)
            for k in range(KT):
                for n in range(2):
                    ins = pe.transpose(ps[k][:, n * P:(n + 1) * P], memx[:, n, k * P:(k + 1) * P], ident[:])
                ins.then_inc(pe_groups, 1)
            phase("memkv")
            w0, a0 = AT["memkv"][3], AT["memkv"][1]
            with pe.Fori(0, 4) as i:
                for j in range(2):
                    pe.wait_ge(w_split, i * 2 + w0 + j + 1)
                    token_panel((w0 + j) % 2, 2 * j, mhi, mlo, 2, wait_free=lambda t: pe.wait_ge(act_freed, i * 4 + a0 + 2 * j + t - 3))
            phase("kt")
            pe.wait_ge(kn_ready, 1)
            for q in range(4):
                for k in range(2):
                    for n in range(2):
                        c = 2 * q + k
                        ins = pe.transpose(ps[q][:, k * MEM + n * P:k * MEM + (n + 1) * P], kraw[:, n, c * P:(c + 1) * P], ident[:])
                ins.then_inc(pe_groups, 1)

            phase("h2")
            prep("h2", lambda t, k: xn[:, t, k * P:(k + 1) * P], 9)
            phase("q")
            w0, a0, d0 = AT["q"][3], AT["q"][1], AT["q"][2]
            with pe.Fori(0, 2) as i:
                for j in range(2):
                    pe.wait_ge(w_split, i * 2 + w0 + j + 1)
                    feature_panel((w0 + j) % 2, 0, wait_free=lambda g: pe.wait_ge(act_freed, i * 8 + a0 + 4 * j + g - 3))
                    pe.wait_ge(q_squared, i * 8 + 4 * j + 4)
                    pe.wait_ge(dve_freed, i * 2 + d0 + j)
                    for t in range(TT):
                        for f in range(2):
                            ins = pe.matmul(ps[4][:, t:t + 1], qsq[:, 2 * f + t // 4, (t % 4) * P:(t % 4 + 1) * P], ones1[:, 0:1],
                                            start=(f == 0), stop=(f == 1))
                    ins.then_inc(pe_groups, 1)

            phase("xatt")

            def mscores(t):
                if t >= 2:
                    pe.wait_ge(c_e, t - 1)
                b = 2 * (t % 2)
                for h in range(4):
                    for f in range(2):
                        ins = pe.matmul(ps[b + h // 2][:, (h % 2) * MEM:(h % 2 + 1) * MEM], qt[:, 2 * h + f, t * P:(t + 1) * P],
                                        khat[:, 2 * h + f, :], start=(f == 0), stop=(f == 1))
                ins.then_inc(c_s, 1)

            mscores(0)
            for t in range(TT):
                if t + 1 < TT:
                    mscores(t + 1)
                pe.wait_ge(c_p, t + 1)
                if t >= 1:
                    pe.wait_ge(c_pt, t)
                for h in range(4):
                    for n in range(2):
                        q = 2 * h + n
                        ins = pe.transpose(ps[4 + q // 4][:, (q % 4) * P:(q % 4 + 1) * P], prob[:, h, n * P:(n + 1) * P], ident[:])
                ins.then_inc(c_t, 1)
                pe.wait_ge(c_pt, t + 1)
                if t >= 1:
                    pe.wait_ge(c_lo, t)
                for k in range(KT):
                    for n in range(2):
                        ins = pe.matmul(ps[6 + k // 4][:, (k % 4) * P:(k % 4 + 1) * P], vmem[:, n, k * P:(k + 1) * P],
                                        probt[:, 2 * (k // 2) + n, :], start=(n == 0), stop=(n == 1))
                ins.then_inc(c_o, 1)

            pe.wait_ge(c_lo, TT)
            token_phase("wmo", dve_freed, AT["wmo"][2])
            phase("h3")
            prep("h3", lambda t, k: xn[:, t, k * P:(k + 1) * P], 17)

            phase("ffn")

            def down(slot, wait_free):
                dn_hi = whi[slot][:].rearrange("p (k a) n -> p k (a n)", k=2)
                dn_lo = wlo[slot][:].rearrange("p (k a) n -> p k (a n)", k=2)
                for t in range(TT):
                    for cc in range(2):
                        g = 2 * t + cc
                        wait_free(g)
                        for k in range(2):
                            tk = slice(t * P, (t + 1) * P)
                            cs = slice(cc * HALF, (cc + 1) * HALF)
                            ins = three(ps[(4 + g) % 8], fhi[:, k, tk], flo[:, k, tk], dn_hi[:, k, cs], dn_lo[:, k, cs],
                                        k == 0, k == 1)
                        ins.then_inc(pe_groups, 1)

            pe.wait_ge(w_split, FFN_W + 1)
            feature_panel(0, 0)
            pe.wait_ge(w_split, FFN_W + 2)
            feature_panel(1, 4)
            with pe.Fori(0, NCH - 1) as i:
                pe.wait_ge(w_split, i * 3 + FFN_W + 3)
                pe.wait_ge(act_freed, i * 4 + FFN_A + 4)
                feature_panel(2, 0, wait_free=lambda g: pe.wait_ge(dve_freed, i * 16 + FFN_D - 3 + g))
                pe.wait_ge(w_split, i * 3 + FFN_W + 4)
                pe.wait_ge(f_lo, i * 4 + 4)

                def down_free(g):
                    if 4 <= g < 8:
                        pe.wait_ge(act_freed, i * 4 + FFN_A + 4 + g - 3)
                    elif g >= 8:
                        pe.wait_ge(dve_freed, i * 16 + FFN_D + g - 7)

                down(0, down_free)
                pe.wait_ge(w_split, i * 3 + FFN_W + 5)
                feature_panel(1, 4, wait_free=lambda g: pe.wait_ge(dve_freed, i * 16 + FFN_D + 9 + g))
            pe.wait_ge(w_split, FFN_W + 3 * NCH)
            pe.wait_ge(f_lo, 4 * NCH)
            dl = FFN_D + 16 * (NCH - 1)
            down(2, lambda g: pe.wait_ge(dve_freed, dl if g < 8 else dl + g - 7))

        @block.scalar
        def _(act):
            st = Steps(act, act_step)

            def stats(srcs, junk, base, n, scale, ready):
                for j, s in enumerate(srcs):
                    st.mark(act.activation(junk(j), s, ACT.Square, accum_out=ssq[:, base + j:base + j + 1]))
                st.settle()
                inverse_root(base, n, scale, ready)

            def inverse_root(base, n, scale, ready):
                st.mark(act.activation(lnv[:, base:base + n], ssq[:, base:base + n], ACT.Ln, bias=EPS, scale=scale))
                st.settle()
                act.activation(rstd[:, base:base + n], lnv[:, base:base + n], ACT.Exp, scale=-0.5).then_inc(ready, 1)

            def prep(name, col, dst=hhi, cols=HALF, halves=2, k_col=None):
                g0 = AT[name][0]
                for hf in range(halves):
                    for k in range(KT):
                        g = hf * KT + k
                        act.wait_ge(pe_groups, g0 + g + 1)
                        wc = k_col(k) if k_col else col + k
                        act.activation(dst[:, k, hf * cols:(hf + 1) * cols], ps[g % 8][:, 0:cols], ACT.Identity,
                                       scale=wcols[:, wc:wc + 1]).then_inc(hi_ready, 1)

            act.preload_act_table_set("natural_log_exp_and_others")
            act.wait_ge(wcols_turned, 1)
            act.activation(wcols[:], ps[7][:, 0:40], ACT.Copy).then_inc(wcols_ready, 1)
            for hf in range(2):
                act.wait_ge(x_landed[hf], 64)
                stats([xres[:, 4 * hf + n, :] for n in range(4)], lambda j: xn[:, 4 * hf + j, :], 4 * hf, 4, 1.0 / D, rstd_ready)
            act.wait_ge(wcols_ready, 1)
            prep("h1", WC_MIX)

            g0 = AT["qkg"][0]
            for j in range(8):
                act.wait_ge(pe_groups, g0 + j + 1)
                dst = (qg if j < 4 else kg)[:, (j % 4) // 2, (j % 2) * HALF:(j % 2 + 1) * HALF]
                act.activation(dst, ps[j], ACT.Copy, scale=GDK ** -0.5 if j < 4 else 1.0).then_inc(act_freed, 1)
            for hf in range(2):
                act.wait_ge(pe_groups, AT["gk"][0] + hf + 1)
                act.activation(lrt[:, hf * HALF:(hf + 1) * HALF], ps[hf][0:16, :], ACT.Copy).then_inc(act_freed, 1)
            for j in range(4):
                act.wait_ge(pe_groups, AT["gkpre"][0] + j + 1)
                act.activation(bsum[:, j // 2, (j % 2) * HALF:(j % 2 + 1) * HALF], ps[j], ACT.Identity,
                               bias=wcols[:, WC_BGK + j // 2:WC_BGK + j // 2 + 1]).then_inc(act_freed, 1)
            act.wait_ge(act_freed, AT["gkpre"][1] + 4)
            st.mark(act.activation(gtmp[:], bsum[:], ACT.Abs))
            st.settle()
            st.mark(act.activation(gtmp[:], gtmp[:], ACT.Exp, scale=-1.0))
            st.settle()
            act.activation(gtmp[:], gtmp[:], ACT.Ln, bias=1.0).then_inc(g_log, 1)
            g0 = AT["gv"][0]
            for n, (dst, f) in enumerate(((gout, ACT.Silu), (vg, ACT.Copy))):
                with act.Fori(0, 2) as i:
                    for t in range(TT):
                        act.wait_ge(pe_groups, i * 8 + g0 + 16 * n + t + 1)
                        act.activation(dst[:, t, ds(i * PW, PW)], ps[t][:, 0:PW], f).then_inc(act_freed, 1)

            act.preload_act_table_set("natural_log_exp_and_others")

            def gla_exps(c, b):
                act.wait_ge(g_x, c + 1)
                act.activation(kx[b][:], kx[b][:], ACT.Exp, scale=1.0 / 16)
                act.activation(qx[b][:, 0:3:2], qx[b][:, 0:3:2], ACT.Exp, scale=1.0 / 16)
                act.activation(qx[b][:, 1], bsum[:, :, ds(c * P, P)], ACT.Exp, scale=1.0 / 16)
                act.activation(decay[b][:], bsum[:, :, ds(c * P + P - 1, 1)].rearrange("p a b -> p (a b)"), ACT.Exp,
                               scale=1.0 / 16).then_inc(g_e, 1)

            def gla_kdt(c):
                act.wait_ge(g_t, c + 1)
                act.activation(kdt[:], ps[2][:, 0:2 * P], ACT.Copy).then_inc(g_kd, 1)

            def gla_turn(c, b, more):
                if more:
                    gla_exps(c + 1, 1 - b)
                act.wait_ge(g_o, c + 1)
                stats([ps[5 + h % 2][:, h // 2 * GDV:(h // 2 + 1) * GDV] for h in range(GH)],
                      lambda j: gsq[:, j * GDV:(j + 1) * GDV], 0, GH, 1.0 / GDV, g_r)
                if more:
                    gla_kdt(c + 1)

            gla_exps(0, 0)
            gla_kdt(0)
            with act.Fori(0, TT - 2, 2) as c:
                st.enter(c, 10, 2)
                gla_turn(c, 0, True)
                gla_turn(c + 1, 1, True)
                st.leave((TT - 2) // 2)
            gla_turn(TT - 2, 0, True)
            gla_turn(TT - 1, 1, False)

            act.wait_ge(g_out, TT)
            g0 = AT["qks"][0]
            for n, (dst, sc) in enumerate(((qs, 64 ** -0.5), (ks, 1.0))):
                for j in range(8):
                    act.wait_ge(pe_groups, g0 + 8 * n + j + 1)
                    act.activation(dst[:, j // 2, (j % 2) * HALF:(j % 2 + 1) * HALF], ps[j], ACT.Copy,
                                   scale=sc).then_inc(act_freed, 1)
            g0 = AT["vs"][0]
            with act.Fori(0, 2) as i:
                for t in range(TT):
                    act.wait_ge(pe_groups, i * 8 + g0 + t + 1)
                    act.activation(vs[:, t, ds(i * PW, PW)], ps[t][:, 0:PW], ACT.Copy).then_inc(act_freed, 1)

            zb = [ps_all[:, 2 * b:2 * b + 2, :].rearrange("p b c -> p (b c)") for b in range(3)]
            with act.Fori(0, 4) as i:
                st.enter(i, 16 + 2)

                def softplus_part(m):
                    c0 = (7 - m % 8) * P
                    act.wait_ge(st_a, i * 16 + m + 1)
                    e = el[m % 3][:, c0:SEQ]
                    st.mark(act.activation(e, e, ACT.Exp))
                    st.settle()
                    act.activation(e, e, ACT.Ln, bias=1.0).then_inc(st_l, 1)

                def weights(m):
                    c0 = (7 - m % 8) * P
                    if m >= 2:
                        act.wait_ge(st_av, i * 16 + m - 1)
                    act.wait_ge(st_arg, i * 16 + m + 1)
                    act.activation(att[m % 2][:, c0:SEQ], zb[m % 3][:, c0:SEQ], ACT.Exp).then_inc(st_att, 1)

                def head_squares(r):
                    act.wait_ge(st_av, i * 16 + 8 * r + 8)
                    act.activation(osq[:], ps[6 + r], ACT.Square).then_inc(st_sq, 1)

                def head_rstd(r):
                    act.wait_ge(st_ss, i * 2 + r + 1)
                    inverse_root(8, 8, 1.0 / 64, st_r)

                softplus_part(0)
                for m in range(16):
                    if m < 15:
                        softplus_part(m + 1)
                    weights(m)
                    if m == 9:
                        head_squares(0)
                    if m == 10:
                        head_rstd(0)
                head_squares(1)
                head_rstd(1)
                st.leave(4)

            prep("mix", 0, k_col=lambda k: WC_GLA if k < 4 else WC_SB)

            act.wait_ge(mem_landed, 16)
            act.wait_ge(dve_freed, AT["mem"][2])
            stats([memx[:, n, :] for n in range(2)], lambda j: kraw[:, j, :], 16, 2, 1.0 / D, rstd_ready)
            prep("mem", WC_MEM, dst=mhi, cols=MEM, halves=1)
            g0 = AT["memkv"][0]
            for n, dst in enumerate((kraw, vmem)):
                with act.Fori(0, 2) as i:
                    for j in range(4):
                        act.wait_ge(pe_groups, i * 4 + g0 + 8 * n + j + 1)
                        act.activation(dst[:, j % 2, ds(i * 2 * PW + (j // 2) * PW, PW)], ps[j][:, 0:PW],
                                       ACT.Copy).then_inc(act_freed, 1)
                if n == 0:
                    act.wait_ge(act_freed, AT["memkv"][1] + 8)
                    stats([kraw[:, n2, h * PW:(h + 1) * PW] for n2 in range(2) for h in range(4)],
                          lambda j: ksq[:, j, :], 0, 8, 1.0 / 256, rstd_ready)
            for q in range(4):
                act.wait_ge(pe_groups, AT["kt"][0] + q + 1)
                for k in range(2):
                    ins = act.activation(khat[:, 2 * q + k, :], ps[q][:, k * MEM:(k + 1) * MEM], ACT.Identity,
                                         scale=kcomb[:, k:k + 1])
                ins.then_inc(act_freed, 1)

            for hf in range(2):
                stats([xres[:, 4 * hf + n, :] for n in range(4)], lambda j: xn[:, 4 * hf + j, :], 4 * hf, 4, 1.0 / D, rstd_ready)
            prep("h2", WC_XA)
            g0 = AT["q"][0]
            with act.Fori(0, 4) as i:
                for j in range(4):
                    act.wait_ge(pe_groups, i * 5 + g0 + j + 1)
                    act.activation(qt[:, ds(i * 2 + j // 2, 1), (j % 2) * HALF:(j % 2 + 1) * HALF], ps[j],
                                   ACT.Copy).then_inc(act_freed, 1)
            act.wait_ge(dve_freed, AT["q"][2] + 4)
            inverse_root(0, 32, 1.0 / 256, rq_ready)
            act.wait_ge(rq_ready, 1)
            for t in range(TT):
                act.wait_ge(c_nb, t + 1)
                if t >= 1:
                    act.wait_ge(c_t, t)
                b = 2 * (t % 2)
                for h in range(4):
                    ins = act.activation(prob[:, h, :], ps[b + h // 2][:, (h % 2) * MEM:(h % 2 + 1) * MEM], ACT.Exp,
                                         bias=mxs[:, 4 + h:5 + h], scale=rstd[:, h * 8 + t:h * 8 + t + 1],
                                         accum_out=mxs[:, 8 + h:9 + h])
                ins.then_inc(c_e, 1)
                act.wait_ge(c_t, t + 1)
                act.activation(probt[:], ps_all[:, 4:6, :].rearrange("p b c -> p (b c)"), ACT.Copy).then_inc(c_pt, 1)
                act.wait_ge(c_o, t + 1)
                for n in range(2):
                    act.activation(hhi[:, 4 * n:4 * n + 4, t * P:(t + 1) * P], ps[6 + n].rearrange("p (k c) -> p k c", k=4), ACT.Identity).then_inc(hi_ready, 1)

            act.wait_ge(dve_freed, AT["h3"][2])
            for hf in range(2):
                stats([xres[:, 4 * hf + n, :] for n in range(4)], lambda j: xn[:, 4 * hf + j, :], 4 * hf, 4, 1.0 / D, rstd_ready)
            prep("h3", WC_FFN)

            def gates(first):
                for g in range(4):
                    act.wait_ge(pe_groups, first + g + 1)
                    act.activation(fgate[:, g, :], ps[g], ACT.Silu).then_inc(act_freed, 1)

            def hidden_hi(first):
                for g in range(4):
                    act.wait_ge(f_hid, first + g + 1)
                    act.activation(fhi[:, g // 2, (g % 2) * HALF:(g % 2 + 1) * HALF], fhid[:, g, :], ACT.Copy).then_inc(f_hi, 1)

            gates(FFN_G)
            hidden_hi(0)
            with act.Fori(0, NCH - 1) as i:
                act.wait_ge(f_hid, i * 4 + 4)
                gates(i * 24 + FFN_G + 8)
                hidden_hi(i * 4 + 4)

        @block.vector
        def _(dve):
            st = Steps(dve, dve_step)

            def prep(name, col, hi0, hi=hhi, lo=hlo, cols=HALF, halves=2, k_col=None):
                for hf in range(halves):
                    for k in range(KT):
                        g = hf * KT + k
                        dve.wait_ge(hi_ready, hi0 + g + 1)
                        wc = k_col(k) if k_col else col + k
                        c = slice(hf * cols, (hf + 1) * cols)
                        dve.scalar_tensor_tensor(out=lo[:, k, c], in0=ps[g % 8][:, 0:cols], scalar=wcols[:, wc:wc + 1],
                                                 in1=hi[:, k, c].bitcast(F32), op0=ALU.mult,
                                                 op1=ALU.subtract).then_inc(dve_freed, 1)

            def normalise(ready0, src, dst):
                for hf in range(2):
                    dve.wait_ge(rstd_ready, ready0 + hf + 1)
                    for t in range(4 * hf, 4 * hf + 4):
                        dve.tensor_scalar(dst[:, t, :], src[:, t, :], rstd[:, t:t + 1], None, ALU.mult).then_inc(xn_ready, 1)

            def add_panels(name):
                g0 = AT[name][0]
                with dve.Fori(0, 4) as i:
                    for t in range(TT):
                        dve.wait_ge(pe_groups, i * 8 + g0 + t + 1)
                        acc = xres[:, t, ds(i * PW, PW)]
                        dve.tensor_tensor(acc, ps[t][:, 0:PW], acc, ALU.add).then_inc(dve_freed, 1)

            normalise(0, xres, xres)
            dve.wait_ge(wcols_ready, 1)
            prep("h1", WC_MIX, 0)

            dve.memset(state[:], 0.0).then_inc(g_s, 1)
            dve.wait_ge(g_log, 1)
            for pr in range(2):
                st.mark(dve.scalar_tensor_tensor(out=gtmp[:, pr, :], in0=bsum[:, pr, :], scalar=0.0, in1=gtmp[:, pr, :],
                                                 op0=ALU.min, op1=ALU.subtract))
            st.settle()
            for pr in range(2):
                for c in range(TT):
                    cc = slice(c * P, (c + 1) * P)
                    st.mark(dve.tensor_tensor_scan(out=bsum[:, pr, cc], data0=gtmp[:, pr, cc], data1=gtmp[:, pr, cc],
                                                   initial=0.0, op0=ALU.add, op1=ALU.bypass))
            st.settle()

            dve.wait_ge(consts_ready, 1)

            def gla_exponents(c, b):
                bt = bsum[:, :, ds(c * P, P)]
                ref = bsum[:, :, ds(c * P + SBK // 2 - 1, P - SBK // 2 + 1)][:, :, 0:P - SBK + 1:SBK]
                last = bsum[:, :, ds(c * P + P - 1, 1)]
                st.mark(dve.tensor_tensor(kx[b][:], ref.unsqueeze(3).to_broadcast([P, 2, NSB, P]),
                                          bt.unsqueeze(2).to_broadcast([P, 2, NSB, P]), ALU.subtract))
                st.mark(dve.tensor_tensor(qx[b][:, 0].rearrange("p a (s j) -> p a s j", j=SBK),
                                          bt.rearrange("p a (s j) -> p a s j", j=SBK),
                                          ref.unsqueeze(3).to_broadcast([P, 2, NSB, SBK]), ALU.subtract))
                st.mark(dve.tensor_tensor(qx[b][:, 2], last.to_broadcast([P, 2, P]), bt, ALU.subtract))
                st.settle()
                dve.tensor_scalar(kx[b][:], kx[b][:], GCLAMP, None, ALU.min)
                dve.tensor_scalar(qx[b][:, 0], qx[b][:, 0], GCLAMP, None, ALU.min).then_inc(g_x, 1)

            def gla_decayed(c, b):
                dve.wait_ge(g_e, c + 1)
                kc, qc = kg[:, :, ds(c * P, P)], qg[:, :, ds(c * P, P)]
                dve.tensor_tensor(kx[b][:], kx[b][:], kc.unsqueeze(2).to_broadcast([P, 2, NSB, P]), ALU.mult)
                dve.tensor_tensor(qx[b][:, 0:2], qx[b][:, 0:2], qc.unsqueeze(1).to_broadcast([P, 2, 2, P]), ALU.mult)
                dve.tensor_tensor(qx[b][:, 2], qx[b][:, 2], kc, ALU.mult).then_inc(g_m, 1)

            def gla_turn(c, b, more):
                if more:
                    gla_exponents(c + 1, 1 - b)
                dve.wait_ge(g_a, c + 1)
                for r in range(2):
                    ins = dve.tensor_tensor(at_sb[:, r], ps[r][:, 0:2 * P].rearrange("p (a i) -> p a i", a=2),
                                            gmask[:].unsqueeze(1).to_broadcast([P, 2, P]), ALU.mult)
                ins.then_inc(g_at, 1)
                if more:
                    gla_decayed(c + 1, 1 - b)
                dve.wait_ge(g_kv, c + 1)
                for pr in range(2):
                    for r in range(2):
                        rows = slice(64 * r, 64 * r + 64)
                        ins = dve.scalar_tensor_tensor(out=state[rows, pr, :], in0=state[rows, pr, :],
                                                       scalar=decay[b][rows, pr:pr + 1],
                                                       in1=ps[3 + pr][rows, r * GDV:(r + 1) * GDV],
                                                       op0=ALU.mult, op1=ALU.add)
                ins.then_inc(g_s, 1)
                dve.wait_ge(g_r, c + 1)
                for h in range(GH):
                    g = gout[:, ds(c, 1), h * GDV:(h + 1) * GDV]
                    ins = dve.scalar_tensor_tensor(out=g, in0=ps[5 + h % 2][:, h // 2 * GDV:(h // 2 + 1) * GDV].unsqueeze(1),
                                                   scalar=rstd[:, h:h + 1], in1=g, op0=ALU.mult, op1=ALU.mult)
                ins.then_inc(g_out, 1)

            gla_exponents(0, 0)
            gla_decayed(0, 0)
            with dve.Fori(0, TT - 2, 2) as c:
                st.enter(c, 6, 2)
                gla_turn(c, 0, True)
                gla_turn(c + 1, 1, True)
                st.leave((TT - 2) // 2)
            gla_turn(TT - 2, 0, True)
            gla_turn(TT - 1, 1, False)

            zb = [ps_all[:, 2 * b:2 * b + 2, :].rearrange("p b c -> p (b c)") for b in range(3)]
            dve.wait_ge(act_freed, AT["stick"][1])
            with dve.Fori(0, 4) as i:
                st.enter(i, 42)

                def bounded(m):
                    c0 = (7 - m % 8) * P
                    dve.wait_ge(st_z, i * 16 + m + 1)
                    dve.tensor_scalar(el[m % 3][:, c0:SEQ], zb[m % 3][:, c0:SEQ], LINEAR, None, ALU.min).then_inc(st_a, 1)

                def softplus(m):
                    c0 = (7 - m % 8) * P
                    s = sp_[m % 2]
                    dve.wait_ge(st_l, i * 16 + m + 1)
                    if m >= 2:
                        dve.wait_ge(st_arg, i * 16 + m - 1)
                    st.mark(dve.tensor_tensor(s[:, c0:SEQ], zb[m % 3][:, c0:SEQ], el[m % 3][:, c0:SEQ], ALU.max))
                    st.settle()
                    dg = s[:, c0:c0 + P]
                    dve.tensor_tensor(dg, dg, smask[:], ALU.mult).then_inc(st_sp, 1)

                def sum_later(m):
                    c0 = (7 - m % 8) * P
                    dve.wait_ge(st_sp, i * 16 + m + 1)
                    if m >= 2:
                        dve.wait_ge(st_arg, i * 16 + m)
                    if m % 8 > 0:
                        st.mark(dve.tensor_tensor(later[m % 2][:, c0 + P:SEQ], later[(m - 1) % 2][:, c0 + P:SEQ],
                                                  sp_[m % 2][:, c0 + P:SEQ], ALU.add))
                    st.mark(dve.tensor_copy(later[m % 2][:, c0:c0 + P], sp_[m % 2][:, c0:c0 + P]))
                    st.settle()

                def head_sums(r):
                    dve.wait_ge(st_sq, i * 2 + r + 1)
                    dve.tensor_reduce(ssq[:, 8:16], osq[:].rearrange("p (t d) -> p t d", d=64), AX.X, ALU.add).then_inc(st_ss, 1)

                def head_out(r):
                    dve.wait_ge(st_r, i * 2 + r + 1)
                    dve.tensor_tensor(os_[:, :, ds(i * P + 64 * r, 64)], ps[6 + r].rearrange("p (t d) -> p t d", d=64),
                                      rstd[:, 8:16].unsqueeze(2).to_broadcast([P, TT, 64]), ALU.mult).then_inc(st_o, 1)

                dve.tensor_copy(qcur[:], qs[:, ds(i, 1), :].rearrange("p a b -> p (a b)"))
                dve.tensor_copy(kcur[:], ks[:, ds(i, 1), :].rearrange("p a b -> p (a b)")).then_inc(st_kq, 1)
                bounded(0)
                for m in range(16):
                    softplus(m)
                    if m < 15:
                        bounded(m + 1)
                    if m % 8 < 7:
                        sum_later(m)
                    if m == 10:
                        head_sums(0)
                    if m == 11:
                        head_out(0)
                head_sums(1)
                head_out(1)
                st.leave(4)

            hi_n = 16
            prep("mix", 0, hi_n, k_col=lambda k: WC_GLA if k < 4 else WC_SB)
            hi_n += 16
            dve.wait_ge(xr_landed, 16 * TT)
            add_panels("wout")
            dve.wait_ge(rstd_ready, 3)
            for n in range(2):
                ins = dve.tensor_scalar(memx[:, n, :], memx[:, n, :], rstd[:, 16 + n:17 + n], None, ALU.mult)
            ins.then_inc(xn_ready, 1)
            prep("mem", WC_MEM, hi_n, hi=mhi, lo=mlo, cols=MEM, halves=1)
            hi_n += 8
            st.mark(dve.tensor_tensor(kcomb[:], wcols[:, WC_MQ:WC_MQ + 2], wcols[:, WC_MK:WC_MK + 2], ALU.mult))
            st.settle()
            st.mark(dve.tensor_scalar(kcomb[:], kcomb[:], 1.0 / 16, None, ALU.mult))
            st.settle()
            dve.wait_ge(rstd_ready, 4)
            for n in range(2):
                for h in range(4):
                    kk = kraw[:, n, h * PW:(h + 1) * PW]
                    ins = dve.tensor_scalar(kk, kk, rstd[:, 4 * n + h:4 * n + h + 1], None, ALU.mult)
            ins.then_inc(kn_ready, 1)
            dve.wait_ge(act_freed, AT["h2"][1])
            normalise(4, xres, xn)
            prep("h2", WC_XA, hi_n)
            hi_n += 16
            with dve.Fori(0, 4) as i:
                for j in range(4):
                    dve.wait_ge(act_freed, i * 4 + AT["q"][1] + j + 1)
                    if j == 0:
                        dve.wait_ge(pe_groups, i * 5 + AT["q"][0])
                    qq = qt[:, ds(i * 2 + j // 2, 1), (j % 2) * HALF:(j % 2 + 1) * HALF]
                    dve.tensor_tensor(qsq[:, j:j + 1, :], qq, qq, ALU.mult).then_inc(q_squared, 1)
                dve.wait_ge(pe_groups, i * 5 + AT["q"][0] + 5)
                dve.tensor_copy(ssq[:, ds(i * 8, 8)], ps[4][:, 0:8]).then_inc(dve_freed, 1)
            dve.wait_ge(rq_ready, 1)
            rq = rstd[:].rearrange("p (h t) -> p h t", t=8)

            def maxima(t):
                dve.wait_ge(c_s, t + 1)
                if t >= 1:
                    dve.wait_ge(c_e, t)
                b = 2 * (t % 2)
                st.mark(dve.tensor_reduce(mxs[:, 0:4], ps_all[:, b:b + 2, :].rearrange("p b (h m) -> p (b h) m", h=2),
                                          AX.X, ALU.max))
                st.settle()
                dve.scalar_tensor_tensor(out=mxs[:, 4:8], in0=mxs[:, 0:4], scalar=-1.0, in1=rq[:, :, t],
                                         op0=ALU.mult, op1=ALU.mult).then_inc(c_nb, 1)

            maxima(0)
            for t in range(TT):
                dve.wait_ge(c_e, t + 1)
                st.mark(dve.reciprocal(mxs[:, 12:16], mxs[:, 8:12]))
                st.settle()
                dve.tensor_tensor(prob[:], prob[:], mxs[:, 12:16].unsqueeze(2).to_broadcast([P, 4, MEM]), ALU.mult).then_inc(c_p, 1)
                if t + 1 < TT:
                    maxima(t + 1)
                for n in range(2):
                    dve.wait_ge(hi_ready, hi_n + 2 * t + n + 1)
                    tk = slice(t * P, (t + 1) * P)
                    ins = dve.tensor_tensor(hlo[:, 4 * n:4 * n + 4, tk], ps[6 + n].rearrange("p (k c) -> p k c", k=4),
                                            hhi[:, 4 * n:4 * n + 4, tk].bitcast(F32), ALU.subtract)
                ins.then_inc(c_lo, 1)
            hi_n += 2 * TT
            add_panels("wmo")
            normalise(6, xres, xn)
            prep("h3", WC_FFN, hi_n)

            def hidden(first_group, act_first, n_first):
                for g in range(4):
                    dve.wait_ge(pe_groups, first_group + g + 1)
                    dve.wait_ge(act_freed, act_first + g + 1)
                    dve.tensor_tensor(fhid[:, g, :], ps[4 + g], fgate[:, g, :], ALU.mult).then_inc(f_hid, 1)
                for g in range(4):
                    dve.wait_ge(f_hi, n_first + g + 1)
                    c = slice((g % 2) * HALF, (g % 2 + 1) * HALF)
                    dve.tensor_tensor(flo[:, g // 2, c], fhid[:, g, :], fhi[:, g // 2, c].bitcast(F32),
                                      ALU.subtract).then_inc(f_lo, 1)

            def add_down(first_group):
                for g in range(16):
                    t, cc = g // 2, g % 2
                    dve.wait_ge(pe_groups, first_group + g + 1)
                    acc = xres[:, t, cc * HALF:(cc + 1) * HALF]
                    dve.tensor_tensor(acc, ps[(4 + g) % 8], acc, ALU.add).then_inc(dve_freed, 1)

            hidden(FFN_G + 4, FFN_A, 0)
            with dve.Fori(0, NCH - 1) as i:
                add_down(i * 24 + FFN_G + 12)
                hidden(i * 24 + FFN_G + 28, i * 4 + FFN_A + 4, i * 4 + 4)
            add_down(FFN_G + 8 + 24 * (NCH - 1))


_INS = ["x", "mem", "mix_norm_w", "w_in", "w_gk_up", "b_gk", "gla_norm_w", "sb_norm_w", "w_out",
        "xattn_norm_w", "mem_norm_w", "w_mq", "w_mkv", "mq_norm_w", "mk_norm_w", "w_mo",
        "ffn_norm_w", "w_gate_up", "w_down"]


def kernel(**inputs):
    import numpy as np
    import concourse.bacc as bacc
    from concourse.bass_utils import run_bass_kernel_spmd

    nc = bacc.Bacc("TRN2", target_bir_lowering=False, num_devices=1)
    arrays, args = {}, []
    for name in _INS:
        a = np.ascontiguousarray(inputs[name])
        arrays[f"in_{name}"] = a
        args.append(nc.dram_tensor(f"in_{name}", a.shape, mybir.dt.from_np(a.dtype), kind="ExternalInput").ap())
    out = nc.dram_tensor("out_0", (1, SEQ, D), F32, kind="ExternalOutput").ap()
    build(nc, *args, out)
    result = run_bass_kernel_spmd(nc, [arrays], core_ids=[0])
    return result.results[0]["out_0"]
```

```python
from contextlib import ExitStack

import concourse.bass as bass
from concourse import mybir

ACT = mybir.ActivationFunctionType
ALU = mybir.AluOpType
AX = mybir.AxisListType
F32 = mybir.dt.float32
F32R = mybir.dt.float32r
BF16 = mybir.dt.bfloat16
ds = bass.ds

P = 128
SEQ = 1024
D = 1024
KT = D // P
TT = SEQ // P
HALF = 512
PW = 256
MEM = 256
DFF = 2816
EPS = 1e-6
GH, GDK, GDV = 4, 64, 128
SBK = 32
NSB = P // SBK
GCLAMP = 38.0 * 16.0
NHEADS_SB = 8
MASKED = -1.0e30
LINEAR = 40.0

COL_QG, COL_KG, COL_VG, COL_GG, COL_GK, COL_QS, COL_KS, COL_VS = 0, 256, 512, 1024, 1536, 1552, 2064, 2576

PHASES = [
    ("h1", 16, 0, 16, 0), ("qkg", 8, 8, 0, 2), ("gk", 2, 2, 0, 1), ("gkpre", 4, 4, 0, 0),
    ("gv", 32, 32, 0, 4), ("gla", 0, 0, 0, 0), ("qks", 16, 16, 0, 4), ("vs", 16, 16, 0, 2),
    ("stick", 0, 0, 0, 0), ("mix", 16, 0, 16, 0), ("mem", 8, 0, 8, 0), ("wout", 32, 0, 32, 4),
    ("memkv", 16, 16, 0, 8), ("kt", 4, 4, 0, 0), ("h2", 16, 0, 16, 0), ("q", 20, 16, 4, 4),
    ("xatt", 0, 0, 0, 0), ("wmo", 32, 0, 32, 4), ("h3", 16, 0, 16, 0), ("ffn", 0, 0, 0, 0),
]
UNITS = []
for key in range(SEQ // P - 1, -1, -1):
    UNITS += [(key, HALF, SEQ), (key, key * P, HALF)] if key * P < HALF else [(key, key * P, SEQ)]
HU = len(UNITS)
HL = sum(key > 0 for key, _, _ in UNITS)
NCH = DFF // PW


def starts():
    at, g, a, d, w = {}, 0, 0, 0, 0
    for name, ng, na, nd, nw in PHASES:
        at[name] = (g, a, d, w)
        g, a, d, w = g + ng, a + na, d + nd, w + nw
    return at


AT = starts()
FFN_G, FFN_A, FFN_D, FFN_W = AT["ffn"]


def panel_ends():
    ends = []
    for name, ng, _, _, nw in PHASES:
        for n in range(nw):
            ends.append(AT[name][0] + ng // nw * (n + 1))
    return ends


PANEL_END = panel_ends()
MKV_W = AT["memkv"][3]
HI_ON_ACT = range(MKV_W, MKV_W + 10)


class Steps:

    def __init__(self, eng, sem):
        self.eng, self.sem, self.done, self.more = eng, sem, 0, 0

    def mark(self, ins):
        ins.then_inc(self.sem, 1)
        self.done += 1

    def settle(self):
        self.eng.wait_ge(self.sem, self.done + self.more)

    def enter(self, i, per, step=1):
        self.first, self.per, self.more = self.done, per, i * (per // step)

    def leave(self, iters):
        assert self.done - self.first == self.per, self.done - self.first
        self.done, self.more = self.first + self.per * iters, 0


def build(nc, x, mem, mix_norm_w, w_in, w_gk_up, b_gk, gla_norm_w, sb_norm_w, w_out,
          xattn_norm_w, mem_norm_w, w_mq, w_mkv, mq_norm_w, mk_norm_w, w_mo,
          ffn_norm_w, w_gate_up, w_down, out):
    x_t = x.rearrange("b (t p) d -> p (b t) d", p=P)
    mem_t = mem.rearrange("b (t p) d -> p (b t) d", p=P)
    out_t = out.rearrange("b (t p) d -> p (b t) d", p=P)

    def weight(w):
        return w.rearrange("l (k p) n -> p (l k) n", p=P)

    win_v, wout_v, wmq_v, wmkv_v, wmo_v, wgu_v, wdn_v = (
        weight(w) for w in (w_in, w_out, w_mq, w_mkv, w_mo, w_gate_up, w_down))

    panels = [(win_v, COL_QG), (win_v, COL_KG), (win_v, COL_GK)]
    panels += [(win_v, COL_GG), (win_v, COL_GG + PW), (win_v, COL_VG), (win_v, COL_VG + PW)]
    panels += [(win_v, c) for c in (COL_QS, COL_QS + PW, COL_KS, COL_KS + PW, COL_VS, COL_VS + PW)]
    panels += [(wout_v, PW * n) for n in range(4)]
    panels += [(wmkv_v, PW * n) for n in range(8)]
    panels += [(wmq_v, PW * n) for n in range(4)]
    panels += [(wmo_v, PW * n) for n in range(4)]
    assert len(panels) == FFN_W == len(PANEL_END)

    with ExitStack() as ctx:
        BASE = 16512

        def at(name, kb, shape, dt=F32):
            return nc.alloc_sbuf_tensor_at(name, shape, dt, offset=BASE + int(kb * 1024))

        def sem(name):
            return ctx.enter_context(nc.semaphore(name))

        raw = [at(f"raw{s}", 8 * s, [P, KT, PW]) for s in range(3)]
        whi = [at(f"whi{s}", 24 + 16 * s, [P, KT, PW], F32R) for s in range(3)]
        wlo = [at(f"wlo{s}", 32 + 16 * s, [P, KT, PW], F32R) for s in range(3)]
        LENT_RAW, LENT = 16, 56
        H = 72
        hhi = at("hhi", H, [P, KT, SEQ], F32R)
        hlo = at("hlo", H + 32, [P, KT, SEQ], F32R)
        M, X = 136, 168
        xres = at("xres", X, [P, TT, D])
        junk_h = at("junk_h", H, [P, TT, D])
        junk_m = at("junk_m", M, [P, TT, D])
        diag = at("diag", LENT_RAW, [P, TT, P])
        C = 200
        ident = at("ident", C, [P, P])
        tri = at("tri", C + 0.5, [P, P])
        nones = at("nones", C + 1, [P, P])
        gmask = at("gmask", C + 1.5, [P, P])
        tri_r = at("tri_r", C + 2, [P, P], F32R)
        negm = at("negm", C + 2.5, [P, P])
        wgu16 = at("wgu16", C + 3, [16, 256])
        wrows = at("wrows", C + 4, [40, P])
        wcols = at("wcols", C + 4.5, [P, 40])
        ones1 = at("ones1", C + 4.75, [P, 4])
        ssq = at("ssq", C + 4.875, [P, 32])
        rstd = at("rstd", C + 5, [P, 32])
        lnv = at("lnv", C + 5.125, [P, 32])
        mxs = at("mxs", C + 5.25, [P, 16])
        kcomb = at("kcomb", C + 5.375, [P, 2])
        ident_b = at("ident_b", C + 5.5, [P, P], BF16)
        negm_b = at("negm_b", C + 5.75, [P, P], BF16)
        ptick = at("ptick", C + 5.4375, [P, 1])
        gout = at("gout", M, [P, TT, 512])
        kx = [at(f"kx{b}", M + 16 + 4 * b, [P, 2, NSB, P]) for b in range(2)]
        bsum = at("bsum", M + 24, [P, 2, SEQ])
        vg = at("vg", X, [P, TT, 512])
        qg = at("qg", X + 16, [P, 2, SEQ])
        kg = at("kg", X + 24, [P, 2, SEQ])
        gtmp = at("gtmp", M + 16, [P, 2, SEQ])
        lrt = at("lrt", LENT, [16, SEQ])
        qx = [at(f"qx{b}", LENT + 3 * b, [P, 3, 2, P]) for b in range(2)]
        at_sb = at("at_sb", LENT + 6, [P, 2, 2, P])
        kdt = at("kdt", LENT + 8, [P, 2 * P])
        state = at("state", LENT + 9, [P, 2, P])
        decay = [at(f"decay{b}", LENT + 10 + 0.125 * b, [P, 2]) for b in range(2)]
        gsq = at("gsq", LENT + 10.5, [P, 512])
        qs = at("qs", M + 16, [P, 4, SEQ])
        ks = at("ks", X, [P, 4, SEQ])
        vs = at("vs", X + 16, [P, TT, 512])
        os_ = at("os_", M + 16, [P, 4, TT, P])
        junk_os = at("junk_os", LENT, [P, 2, D])
        kst = [at(f"kst{r}", LENT + 4 * r, [P, SEQ], F32R) for r in range(2)]
        qst = [at(f"qst{r}", LENT + 8 + 4 * r, [P, SEQ], F32R) for r in range(2)]
        qlo = at("qlo", H + 60, [P, SEQ], F32R)
        el = at("el", H, [P, 6, HALF])
        sphi = [at(f"sphi{b}", H + 12 + 2 * b, [P, HALF], F32R) for b in range(4)]
        splo = [at(f"splo{b}", H + 20 + 2 * b, [P, HALF], F32R) for b in range(4)]
        later = [at(f"later{b}", H + 28 + 4 * b, [P, SEQ]) for b in range(2)]
        att = [at(f"att{b}", H + 36 + 2 * b, [P, HALF]) for b in range(4)]
        memx = at("memx", LENT_RAW, [P, 2, D])
        mhi = at("mhi", M + 16, [P, KT, MEM], F32R)
        mlo = at("mlo", M + 24, [P, KT, MEM], F32R)
        kraw = at("kraw", M, [P, 2, D])
        ksq = at("ksq", M + 8, [P, 8, PW])
        khat = at("khat", LENT, [P, KT, MEM])
        vmem = at("vmem", LENT + 8, [P, 2, D])
        qt = at("qt", M, [P, KT, SEQ])
        qsq = at("qsq", LENT_RAW, [P, 4, HALF])
        prob = at("prob", LENT_RAW, [P, 4, MEM])
        probt = at("probt", LENT_RAW + 4, [P, 8, P])
        fhi = at("fhi", M, [P, 2, SEQ], F32R)
        flo = at("flo", M + 8, [P, 2, SEQ], F32R)
        fgate = at("fgate", M + 16, [P, 4, HALF])
        fhid = at("fhid", M + 24, [P, 4, HALF])

        ps_all = ctx.enter_context(nc.psum_tensor("ps_all", [P, 8, HALF], F32))
        ps = [ps_all[:, b, :] for b in range(8)]

        raw_landed = [sem(f"raw_landed{s}") for s in range(3)]
        w_split = sem("w_split")
        x_landed = [sem(f"x_landed{n}") for n in range(2)]
        xr_landed = sem("xr_landed")
        small_landed = sem("small_landed")
        mem_landed = sem("mem_landed")
        out_landed = sem("out_landed")
        pe_groups, act_freed, dve_freed = sem("pe_groups"), sem("act_freed"), sem("dve_freed")
        consts_ready = sem("consts_ready")
        wcols_turned, wcols_ready = sem("wcols_turned"), sem("wcols_ready")
        rstd_ready, diag_ready, hi_ready = sem("rstd_ready"), sem("diag_ready"), sem("hi_ready")
        mem_scaled, w_hi = sem("mem_scaled"), sem("w_hi")
        act_step, dve_step, pool_step = sem("act_step"), sem("dve_step"), sem("pool_step")
        g_log = sem("g_log")
        g_x, g_e, g_m, g_t, g_a, g_at = (sem(n) for n in ("g_x", "g_e", "g_m", "g_t", "g_a", "g_at"))
        g_kd, g_o, g_kv, g_s, g_r, g_out = (sem(n) for n in ("g_kd", "g_o", "g_kv", "g_s", "g_r", "g_out"))
        st_kq, st_z, st_a, st_l, st_sp = (sem(n) for n in ("st_kq", "st_z", "st_a", "st_l", "st_sp"))
        st_hi, st_lo, st_later = sem("st_hi"), sem("st_lo"), sem("st_later")
        st_arg, st_att, st_av = (sem(n) for n in ("st_arg", "st_att", "st_av"))
        st_sq, st_ss, st_r, st_o = (sem(n) for n in ("st_sq", "st_ss", "st_r", "st_o"))
        kn_ready, q_copied, q_squared = sem("kn_ready"), sem("q_copied"), sem("q_squared")
        rq_ready = sem("rq_ready")
        c_s, c_nb, c_e, c_p, c_t, c_pt = (sem(n) for n in ("c_s", "c_nb", "c_e", "c_p", "c_t", "c_pt"))
        c_o, c_lo = sem("c_o"), sem("c_lo")
        f_hid, f_hi, f_lo = sem("f_hid"), sem("f_hi"), sem("f_lo")

        WC_MIX, WC_XA, WC_MEM, WC_FFN, WC_GLA, WC_SB, WC_MQ, WC_MK, WC_BGK = 0, 8, 16, 24, 32, 33, 34, 36, 38

        assert HU % 6 == 0 and HU % 4 == 0

        def unit(n):
            return UNITS[n % HU]

        def scores_of(n):
            key, a, b = unit(n)
            return ps[n % 6][:, a % HALF:a % HALF + b - a]

        def el_of(n):
            key, a, b = unit(n)
            return el[:, n % 6, a % HALF:a % HALF + b - a]

        def before(n):
            key, a, b = unit(n)
            return n - [d for d in (1, 2) if unit(n - d)[0] == key + 1 and unit(n - d)[2] == b][0]

        class StickPair:

            def __init__(self, i, first=False, past=False):
                self.i, self.first, self.past = i, first, past

            def has(self, n):
                return not (self.first and n < 0) and not (self.past and n >= 0)

            def wait(self, eng, signal, n):
                if not (self.first and n < 0):
                    eng.wait_ge(signal, self.i * (2 * HU) + n + 1)

            def wait_later(self, eng, n):
                in_pair = n % (2 * HU)
                eng.wait_ge(st_later, self.pair(n) * (2 * HL) + in_pair // HU * HL + in_pair % HU + 1)

            def pair(self, n):
                return self.i if n >= 0 else self.i - 1

        def stick(eng, step, counted=None, per=0):
            first = StickPair(0, first=True)
            for k in range(2 * HU):
                step(first, k)
            with eng.Fori(0, 3) as j:
                if counted:
                    counted.enter(j, per)
                for k in range(2 * HU):
                    step(StickPair(j + 1), k)
                if counted:
                    counted.leave(3)
            last = StickPair(4, past=True)
            for k in range(10):
                step(last, k)

        block = ctx.enter_context(nc.Block())

        @block.sync
        def _(sp):
            for hf in range(2):
                for t in range(4 * hf, 4 * hf + 4):
                    sp.dma_start(xres[:, t, :], x_t[:, t, :]).then_inc(x_landed[hf], 16)
                if hf == 0:
                    sp.wait_ge(consts_ready, 1)
                    rows = [(WC_MIX, mix_norm_w), (WC_XA, xattn_norm_w), (WC_MEM, mem_norm_w),
                            (WC_FFN, ffn_norm_w), (WC_GLA, gla_norm_w), (WC_MQ, mq_norm_w),
                            (WC_MK, mk_norm_w), (WC_BGK, b_gk)]
                    for r, w in rows:
                        n = w.shape[1] // P
                        sp.dma_start(wrows[r:r + n, :], w.rearrange("l (r c) -> (l r) c", c=P)).then_inc(small_landed, 16)
                    for j in range(2):
                        sp.dma_start(wrows[WC_SB:WC_SB + 1, 64 * j:64 * j + 64], sb_norm_w).then_inc(small_landed, 16)
                    sp.dma_start(wgu16[:, :], w_gk_up.rearrange("l r c -> (l r) c")).then_inc(small_landed, 16)
            for p, (view, col) in enumerate(panels):
                if p >= 2:
                    sp.wait_ge(w_split, p - 1)
                sp.dma_start(raw[p % 2][:], view[:, :, col:col + PW]).then_inc(raw_landed[p % 2], 16)
                if p == AT["wout"][3] + 1:
                    sp.wait_ge(st_o, NHEADS_SB)
                    for t in range(TT):
                        sp.dma_start(xres[:, t, :], x_t[:, t, :]).then_inc(xr_landed, 16)
                if p == AT["gv"][3]:
                    sp.wait_ge(pe_groups, AT["qkg"][0])
                    sp.dma_start(memx[:], mem_t).then_inc(mem_landed, 16)

            def load_gate(slot, c):
                sp.dma_start(raw[slot][:], wgu_v[:, :, ds(c * PW, PW)]).then_inc(raw_landed[slot], 16)

            def load_up(slot, c):
                sp.dma_start(raw[slot][:], wgu_v[:, :, ds(c * PW + DFF, PW)]).then_inc(raw_landed[slot], 16)

            def load_down(slot, c):
                dst = raw[slot][:].rearrange("p (k a) n -> p k (a n)", k=2)
                sp.dma_start(dst, wdn_v[:, ds(c * 2, 2), :]).then_inc(raw_landed[slot], 16)

            sp.wait_ge(w_split, FFN_W)
            load_gate(0, 0)
            load_up(1, 0)
            sp.wait_ge(dve_freed, FFN_D)
            with sp.Fori(0, NCH - 1) as i:
                sp.wait_ge(w_split, FFN_W + i * 3)
                load_gate(2, i + 1)
                sp.wait_ge(w_split, FFN_W + 1 + i * 3)
                load_down(0, i)
                sp.wait_ge(w_split, FFN_W + 2 + i * 3)
                load_up(1, i + 1)
            sp.wait_ge(w_split, FFN_W + 3 * (NCH - 1))
            load_down(2, NCH - 1)
            for t in range(TT):
                sp.wait_ge(dve_freed, FFN_D + (NCH - 1) * 16 + 2 * t + 2)
                sp.dma_start(out_t[:, t, :], xres[:, t, :]).then_inc(out_landed, 16)
            sp.wait_ge(out_landed, 16 * TT)

        @block.gpsimd
        def _(pool):
            st = Steps(pool, pool_step)
            for t, v in ((ident, 0.0), (tri, -1.0), (nones, -1.0), (gmask, 1.0), (negm, MASKED), (ones1, 1.0)):
                st.mark(pool.memset(t[:], v))
            st.mark(pool.memset(wrows[:], 0.0))
            st.settle()

            def tri_select(t, op, base, mult, step, fill):
                return pool.affine_select(out=t[:], in_=t[:], compare_op=op, fill=fill, base=base,
                                          pattern=[[step, P]], channel_multiplier=mult)

            st.mark(tri_select(ident, ALU.not_equal, 0, 1, -1, 1.0))
            st.mark(tri_select(tri, ALU.is_ge, 0, 1, -1, 0.0))
            st.mark(tri_select(gmask, ALU.is_ge, 0, -1, 1, 0.0))
            st.mark(tri_select(negm, ALU.is_ge, 0, 1, -1, 0.0))
            st.settle()
            st.mark(pool.tensor_copy(tri_r[:], tri[:]))
            st.mark(pool.tensor_copy(ident_b[:], ident[:]))
            pool.tensor_copy(negm_b[:], negm[:]).then_inc(consts_ready, 1)

            def tick():
                st.mark(pool.tensor_tensor(ptick[0:1], ones1[0:1, 0:1], ones1[0:1, 0:1], ALU.mult))

            def settled():
                st.settle()
                tick()

            def stage(i, r):
                own, other = slice(64 * r, 64 * r + 64), slice(64 - 64 * r, 128 - 64 * r)
                kk = ks[own, ds(i, 1), :].rearrange("p a b -> p (a b)")
                qq = qs[own, ds(i, 1), :].rearrange("p a b -> p (a b)")
                st.mark(pool.tensor_copy(kst[r][own], kk))
                settled()
                st.mark(pool.tensor_tensor(kst[r][other], kk, kst[r][own].bitcast(F32), ALU.subtract))
                settled()
                st.mark(pool.tensor_copy(qst[r][own], qq))
                settled()
                st.mark(pool.tensor_copy(qst[r][other], qq))
                settled()
                if isinstance(i, int) and r == 0:
                    pool.wait_ge(act_freed, AT["stick"][1])
                pool.tensor_tensor(qlo[own], qq, qst[r][own].bitcast(F32), ALU.subtract).then_inc(st_kq, 1)
                pool.wait_ge(st_kq, i * 2 + r + 1)
                tick()

            def stage_stick():
                pool.wait_ge(act_freed, AT["vs"][1])
                pool.wait_ge(w_split, AT["wout"][3])
                tick()
                for r in range(2):
                    stage(0, r)
                with pool.Fori(0, 3) as j:
                    st.enter(j, 20)
                    for r in range(2):
                        st.settle()
                        pool.wait_ge(st_z, j * (2 * HU) + HU * r + HU)
                        tick()
                        stage(j + 1, r)
                    st.leave(3)
                st.settle()

            def split(slot):
                tick()
                st.mark(pool.tensor_copy(whi[slot][:], raw[slot][:]))
                st.settle()
                low(slot)

            def low(slot):
                pool.tensor_tensor(wlo[slot][:], raw[slot][:], whi[slot][:].bitcast(F32),
                                   ALU.subtract).then_inc(w_split, 1)

            for p in range(FFN_W):
                if p == AT["wout"][3]:
                    stage_stick()
                pool.wait_ge(raw_landed[p % 2], 16 * (p // 2 + 1))
                if p >= 2:
                    pool.wait_ge(pe_groups, PANEL_END[p - 2])
                if p in HI_ON_ACT:
                    pool.wait_ge(w_hi, p - MKV_W + 1)
                    low(p % 2)
                else:
                    split(p % 2)
            n0, n1 = 16 * ((FFN_W + 1) // 2), 16 * (FFN_W // 2)
            pool.wait_ge(raw_landed[0], n0 + 16)
            pool.wait_ge(pe_groups, PANEL_END[FFN_W - 1])
            split(0)
            pool.wait_ge(raw_landed[1], n1 + 16)
            split(1)
            pool.wait_ge(c_lo, TT)
            with pool.Fori(0, NCH - 1) as i:
                st.enter(i, 6)
                pool.wait_ge(raw_landed[2], i * 16 + 16)
                pool.wait_ge(pe_groups, FFN_G - 12 + i * 24)
                split(2)
                pool.wait_ge(raw_landed[0], i * 16 + n0 + 32)
                pool.wait_ge(pe_groups, FFN_G + 4 + i * 24)
                split(0)
                pool.wait_ge(raw_landed[1], i * 16 + n1 + 32)
                pool.wait_ge(pe_groups, FFN_G + 8 + i * 24)
                split(1)
                st.leave(NCH - 1)
            pool.wait_ge(raw_landed[2], 16 * NCH)
            pool.wait_ge(pe_groups, FFN_G + 8 + (NCH - 2) * 24 + 4)
            split(2)

        @block.tensor
        def _(pe):
            def phase(name):
                _, a, d, _ = AT[name]
                if a:
                    pe.wait_ge(act_freed, a)
                if d:
                    pe.wait_ge(dve_freed, d)

            def prep(name, src, diag_base):
                d0 = AT[name][2]
                for hf in range(2):
                    if diag_base is not None:
                        pe.wait_ge(diag_ready, diag_base + hf + 1)
                    for k in range(KT):
                        g = hf * KT + k
                        if g >= 8:
                            pe.wait_ge(dve_freed, d0 + g - 7)
                        for n in range(4):
                            dst = ps[g % 8][:, n * P:(n + 1) * P]
                            if diag_base is None:
                                ins = pe.transpose(dst, src(4 * hf + n, k), ident[:])
                            else:
                                ins = pe.matmul(dst, src(4 * hf + n, k), diag[:, 4 * hf + n, :], start=True, stop=True)
                        ins.then_inc(pe_groups, 1)

            def three(dst, s_hi, s_lo, m_hi, m_lo, first, last):
                pe.matmul(dst, s_hi, m_hi, start=first, stop=False)
                pe.matmul(dst, s_lo, m_hi, start=False, stop=False)
                return pe.matmul(dst, s_hi, m_lo, start=False, stop=last)

            def feature_panel(slot, bank0, tiles=2, wait_free=None):
                for j in range(tiles):
                    for hf in range(2):
                        g = 2 * j + hf
                        if wait_free is not None:
                            wait_free(g)
                        c = slice(hf * HALF, (hf + 1) * HALF)
                        for k in range(KT):
                            ins = three(ps[bank0 + g], whi[slot][:, k, j * P:(j + 1) * P], wlo[slot][:, k, j * P:(j + 1) * P],
                                        hhi[:, k, c], hlo[:, k, c], k == 0, k == KT - 1)
                        ins.then_inc(pe_groups, 1)

            def token_panel(slot, bank0, a_hi, a_lo, tiles, wait_free=None):
                for t in range(tiles):
                    if wait_free is not None:
                        wait_free(t)
                    for k in range(KT):
                        ins = three(ps[bank0 + t][:, 0:PW], a_hi[:, k, t * P:(t + 1) * P], a_lo[:, k, t * P:(t + 1) * P],
                                    whi[slot][:, k, :], wlo[slot][:, k, :], k == 0, k == KT - 1)
                    ins.then_inc(pe_groups, 1)

            def feature_phase(name):
                _, a0, _, w0 = AT[name]
                n = [nw for nm, _, _, _, nw in PHASES if nm == name][0]
                phase(name)
                with pe.Fori(0, n // 2) as i:
                    for j in range(2):
                        pe.wait_ge(w_split, i * 2 + w0 + j + 1)
                        feature_panel((w0 + j) % 2, 4 * j, wait_free=lambda g: pe.wait_ge(act_freed, i * 8 + a0 + 4 * j + g - 7))

            def token_phase(name, freed, f0):
                w0 = AT[name][3]
                n = [nw for nm, _, _, _, nw in PHASES if nm == name][0]
                phase(name)
                with pe.Fori(0, n // 2) as i:
                    for j in range(2):
                        pe.wait_ge(w_split, i * 2 + w0 + j + 1)
                        token_panel((w0 + j) % 2, 0, hhi, hlo, TT,
                                    wait_free=lambda t: pe.wait_ge(freed, i * 16 + f0 + 8 * j + t - 7))

            pe.wait_ge(consts_ready, 1)
            pe.wait_ge(small_landed, 16 * 11)
            pe.transpose(ps[7][:, 0:40], wrows[:], ident[0:40, 0:40]).then_inc(wcols_turned, 1)

            prep("h1", lambda t, k: xres[:, t, k * P:(k + 1) * P], 0)

            phase("qkg")
            for j in range(2):
                pe.wait_ge(w_split, j + 1)
                feature_panel(j, 4 * j)
            phase("gk")
            pe.wait_ge(w_split, 3)
            feature_panel(0, 0, tiles=1)
            phase("gkpre")
            for pr in range(2):
                for hf in range(2):
                    pe.matmul(ps[2 * pr + hf], wgu16[:, pr * P:(pr + 1) * P], lrt[:, hf * HALF:(hf + 1) * HALF],
                              start=True, stop=True).then_inc(pe_groups, 1)
            token_phase("gv", act_freed, AT["gv"][1])

            phase("gla")

            def gla_scores(c, b):
                pe.wait_ge(g_m, c + 1)
                for pr in range(2):
                    ins = pe.transpose(ps[2][:, pr * P:(pr + 1) * P], qx[b][:, 2, pr, :], ident[:])
                ins.then_inc(g_t, 1)
                for pr in range(2):
                    for r in range(2):
                        rows = slice(64 * r, 64 * r + 64)
                        for s in range(NSB):
                            ins = pe.matmul(ps[r][:, pr * P + s * SBK:pr * P + (s + 1) * SBK], kx[b][rows, pr, s, :],
                                            qx[b][rows, 0, pr, s * SBK:(s + 1) * SBK], start=True, stop=True)
                ins.then_inc(g_a, 1)

            def gla_outputs(c, b):
                pe.wait_ge(g_at, c + 1)
                pe.wait_ge(g_s, c + 1)
                for h in range(GH):
                    pr, r = h // 2, h % 2
                    dst = ps[5 + r][:, pr * GDV:(pr + 1) * GDV]
                    pe.matmul(dst, at_sb[:, r, pr, :], vg[:, ds(c, 1), h * GDV:(h + 1) * GDV],
                              start=(pr == 0), stop=False, skip_group_check=True)
                    rows = slice(64 * r, 64 * r + 64)
                    ins = pe.matmul(dst, qx[b][rows, 1, pr, :], state[rows, pr, :],
                                    start=False, stop=True, skip_group_check=True)
                ins.then_inc(g_o, 1)
                pe.wait_ge(g_kd, c + 1)
                for pr in range(2):
                    ins = pe.matmul(ps[3 + pr][:, 0:2 * GDV], kdt[:, pr * P:(pr + 1) * P],
                                    vg[:, ds(c, 1), pr * 2 * GDV:(pr + 1) * 2 * GDV], start=True, stop=True)
                ins.then_inc(g_kv, 1)

            def gla_turn(c, b, more):
                gla_outputs(c, b)
                if more:
                    gla_scores(c + 1, 1 - b)

            gla_scores(0, 0)
            with pe.Fori(0, TT - 2, 2) as c:
                gla_turn(c, 0, True)
                gla_turn(c + 1, 1, True)
            gla_turn(TT - 2, 0, True)
            gla_turn(TT - 1, 1, False)

            pe.wait_ge(g_out, TT)
            feature_phase("qks")
            token_phase("vs", act_freed, AT["vs"][1])

            phase("stick")

            def scores(sp, n):
                key, a, b = unit(n)
                r = n // HU
                sp.wait(pe, st_att, n - 6)
                if n % HU == 0:
                    pe.wait_ge(st_kq, sp.i * 2 + r + 1)
                own, tile, z = slice(64 * r, 64 * r + 64), slice(key * P, (key + 1) * P), scores_of(n)
                pe.matmul(z, kst[r][:, tile], qst[r][:, a:b], start=True, stop=False, skip_group_check=True)
                ins = pe.matmul(z, kst[r][own, tile], qlo[own, a:b], start=False, stop=False, skip_group_check=True)
                if a == key * P:
                    ins = pe.matmul(z[:, 0:P], ident_b[:], negm_b[:], start=False, stop=False, skip_group_check=True)
                ins.then_inc(st_z, 1)

            def exponent(sp, n):
                key, a, b = unit(n)
                z = scores_of(n)
                sp.wait(pe, st_lo, n)
                c = max(a, (key + 1) * P)
                if c < b:
                    sp.wait_later(pe, before(n))
                    pe.matmul(z[:, c - a:b - a], nones[:], later[(key + 1) % 2][:, c:b],
                              start=False, stop=False, skip_group_check=True)
                pe.matmul(z, tri_r[:], sphi[n % 4][:, 0:b - a], start=False, stop=False, skip_group_check=True)
                pe.matmul(z, tri_r[:], splo[n % 4][:, 0:b - a], start=False, stop=True,
                          skip_group_check=True).then_inc(st_arg, 1)

            def values(sp, n):
                key, a, b = unit(n)
                r = n % (2 * HU) // HU
                sp.wait(pe, st_att, n)
                if n % HU == 0 and not sp.first:
                    pe.wait_ge(st_o, sp.i * 2 - 1 + r)
                for t in range(a // P, b // P):
                    ins = pe.matmul(ps[6 + r][:, t * 64:(t + 1) * 64], att[n % 4][:, t * P - a:(t + 1) * P - a],
                                    vs[:, key, ds(sp.pair(n) * P + 64 * r, 64)],
                                    start=(key == 7), stop=(key == 0), skip_group_check=True)
                ins.then_inc(st_av, 1)

            def stick_step(sp, k):
                if sp.has(k):
                    scores(sp, k)
                if sp.has(k - 6):
                    values(sp, k - 6)
                if sp.has(k - 4):
                    exponent(sp, k - 4)

            stick(pe, stick_step)

            pe.wait_ge(st_o, NHEADS_SB)
            phase("mix")
            prep("mix", lambda t, k: gout[:, t, k * P:(k + 1) * P] if k < 4 else os_[:, k - 4, t, :], None)
            phase("mem")
            pe.wait_ge(mem_scaled, 1)
            for k in range(KT):
                for n in range(2):
                    ins = pe.transpose(ps[k][:, n * P:(n + 1) * P], memx[:, n, k * P:(k + 1) * P], ident[:])
                ins.then_inc(pe_groups, 1)
            token_phase("wout", dve_freed, AT["wout"][2])

            phase("memkv")
            w0, a0 = AT["memkv"][3], AT["memkv"][1]
            with pe.Fori(0, 4) as i:
                for j in range(2):
                    pe.wait_ge(w_split, i * 2 + w0 + j + 1)
                    token_panel((w0 + j) % 2, 2 * j, mhi, mlo, 2, wait_free=lambda t: pe.wait_ge(act_freed, i * 4 + a0 + 2 * j + t - 3))
            phase("kt")
            pe.wait_ge(kn_ready, 1)
            for q in range(4):
                for k in range(2):
                    for n in range(2):
                        c = 2 * q + k
                        ins = pe.transpose(ps[q][:, k * MEM + n * P:k * MEM + (n + 1) * P], kraw[:, n, c * P:(c + 1) * P], ident[:])
                ins.then_inc(pe_groups, 1)

            phase("h2")
            prep("h2", lambda t, k: xres[:, t, k * P:(k + 1) * P], 2)
            phase("q")
            w0, a0, d0 = AT["q"][3], AT["q"][1], AT["q"][2]
            with pe.Fori(0, 2) as i:
                for j in range(2):
                    pe.wait_ge(w_split, i * 2 + w0 + j + 1)
                    feature_panel((w0 + j) % 2, 0, wait_free=lambda g: pe.wait_ge(act_freed, i * 8 + a0 + 4 * j + g - 3))
                    pe.wait_ge(q_squared, i * 8 + 4 * j + 4)
                    pe.wait_ge(dve_freed, i * 2 + d0 + j)
                    for t in range(TT):
                        for f in range(2):
                            ins = pe.matmul(ps[4][:, t:t + 1], qsq[:, 2 * f + t // 4, (t % 4) * P:(t % 4 + 1) * P], ones1[:, 0:1],
                                            start=(f == 0), stop=(f == 1))
                    ins.then_inc(pe_groups, 1)

            phase("xatt")

            def mscores(t):
                if t >= 2:
                    pe.wait_ge(c_e, t - 1)
                b = 2 * (t % 2)
                for h in range(4):
                    for f in range(2):
                        ins = pe.matmul(ps[b + h // 2][:, (h % 2) * MEM:(h % 2 + 1) * MEM], qt[:, 2 * h + f, t * P:(t + 1) * P],
                                        khat[:, 2 * h + f, :], start=(f == 0), stop=(f == 1))
                ins.then_inc(c_s, 1)

            def mturn(t):
                pe.wait_ge(c_p, t + 1)
                if t >= 1:
                    pe.wait_ge(c_pt, t)
                for h in range(4):
                    for n in range(2):
                        q = 2 * h + n
                        ins = pe.transpose(ps[4 + q // 4][:, (q % 4) * P:(q % 4 + 1) * P], prob[:, h, n * P:(n + 1) * P], ident[:])
                ins.then_inc(c_t, 1)

            def mvalues(t):
                pe.wait_ge(c_pt, t + 1)
                if t >= 1:
                    pe.wait_ge(c_lo, t)
                for k in range(KT):
                    for n in range(2):
                        ins = pe.matmul(ps[6 + k // 4][:, (k % 4) * P:(k % 4 + 1) * P], vmem[:, n, k * P:(k + 1) * P],
                                        probt[:, 2 * (k // 2) + n, :], start=(n == 0), stop=(n == 1))
                ins.then_inc(c_o, 1)

            mscores(0)
            for t in range(TT):
                if t + 1 < TT:
                    mscores(t + 1)
                if t >= 1:
                    mvalues(t - 1)
                mturn(t)
            mvalues(TT - 1)

            pe.wait_ge(c_lo, TT)
            token_phase("wmo", dve_freed, AT["wmo"][2])
            phase("h3")
            prep("h3", lambda t, k: xres[:, t, k * P:(k + 1) * P], 4)

            phase("ffn")

            def down(slot, wait_free):
                dn_hi = whi[slot][:].rearrange("p (k a) n -> p k (a n)", k=2)
                dn_lo = wlo[slot][:].rearrange("p (k a) n -> p k (a n)", k=2)
                for t in range(TT):
                    for cc in range(2):
                        g = 2 * t + cc
                        wait_free(g)
                        for k in range(2):
                            tk = slice(t * P, (t + 1) * P)
                            cs = slice(cc * HALF, (cc + 1) * HALF)
                            ins = three(ps[(4 + g) % 8], fhi[:, k, tk], flo[:, k, tk], dn_hi[:, k, cs], dn_lo[:, k, cs],
                                        k == 0, k == 1)
                        ins.then_inc(pe_groups, 1)

            pe.wait_ge(w_split, FFN_W + 1)
            feature_panel(0, 0)
            pe.wait_ge(w_split, FFN_W + 2)
            feature_panel(1, 4)
            with pe.Fori(0, NCH - 1) as i:
                pe.wait_ge(w_split, i * 3 + FFN_W + 3)
                pe.wait_ge(act_freed, i * 4 + FFN_A + 4)
                feature_panel(2, 0, wait_free=lambda g: pe.wait_ge(dve_freed, i * 16 + FFN_D - 3 + g))
                pe.wait_ge(w_split, i * 3 + FFN_W + 4)
                pe.wait_ge(f_lo, i * 4 + 4)

                def down_free(g):
                    if 4 <= g < 8:
                        pe.wait_ge(act_freed, i * 4 + FFN_A + 4 + g - 3)
                    elif g >= 8:
                        pe.wait_ge(dve_freed, i * 16 + FFN_D + g - 7)

                down(0, down_free)
                pe.wait_ge(w_split, i * 3 + FFN_W + 5)
                feature_panel(1, 4, wait_free=lambda g: pe.wait_ge(dve_freed, i * 16 + FFN_D + 9 + g))
            pe.wait_ge(w_split, FFN_W + 3 * NCH)
            pe.wait_ge(f_lo, 4 * NCH)
            dl = FFN_D + 16 * (NCH - 1)
            down(2, lambda g: pe.wait_ge(dve_freed, dl if g < 8 else dl + g - 7))

        @block.scalar
        def _(act):
            st = Steps(act, act_step)

            def stats(srcs, junk, base, n, scale, ready):
                for j, s in enumerate(srcs):
                    st.mark(act.activation(junk(j), s, ACT.Square, accum_out=ssq[:, base + j:base + j + 1]))
                st.settle()
                inverse_root(base, n, scale, ready)

            def inverse_root(base, n, scale, ready):
                st.mark(act.activation(lnv[:, base:base + n], ssq[:, base:base + n], ACT.Ln, bias=EPS, scale=scale))
                st.settle()
                act.activation(rstd[:, base:base + n], lnv[:, base:base + n], ACT.Exp, scale=-0.5).then_inc(ready, 1)

            def token_stats(hf, junk):
                stats([xres[:, 4 * hf + n, :] for n in range(4)], lambda j: junk[:, 4 * hf + j, :], 4 * hf, 4, 1.0 / D, rstd_ready)

            def prep(name, col, dst=hhi, cols=HALF, halves=2, k_col=None):
                g0 = AT[name][0]
                for hf in range(halves):
                    for k in range(KT):
                        g = hf * KT + k
                        act.wait_ge(pe_groups, g0 + g + 1)
                        wc = k_col(k) if k_col else col + k
                        act.activation(dst[:, k, hf * cols:(hf + 1) * cols], ps[g % 8][:, 0:cols], ACT.Identity,
                                       scale=wcols[:, wc:wc + 1]).then_inc(hi_ready, 1)

            act.preload_act_table_set("natural_log_exp_and_others")
            act.wait_ge(wcols_turned, 1)
            act.activation(wcols[:], ps[7][:, 0:40], ACT.Copy).then_inc(wcols_ready, 1)
            for hf in range(2):
                act.wait_ge(x_landed[hf], 64)
                token_stats(hf, junk_h)
            act.wait_ge(wcols_ready, 1)
            prep("h1", WC_MIX)

            g0 = AT["qkg"][0]
            for j in range(8):
                act.wait_ge(pe_groups, g0 + j + 1)
                dst = (qg if j < 4 else kg)[:, (j % 4) // 2, (j % 2) * HALF:(j % 2 + 1) * HALF]
                act.activation(dst, ps[j], ACT.Copy, scale=GDK ** -0.5 if j < 4 else 1.0).then_inc(act_freed, 1)
            for hf in range(2):
                act.wait_ge(pe_groups, AT["gk"][0] + hf + 1)
                act.activation(lrt[:, hf * HALF:(hf + 1) * HALF], ps[hf][0:16, :], ACT.Copy).then_inc(act_freed, 1)
            for j in range(4):
                act.wait_ge(pe_groups, AT["gkpre"][0] + j + 1)
                act.activation(bsum[:, j // 2, (j % 2) * HALF:(j % 2 + 1) * HALF], ps[j], ACT.Identity,
                               bias=wcols[:, WC_BGK + j // 2:WC_BGK + j // 2 + 1]).then_inc(act_freed, 1)
            act.wait_ge(act_freed, AT["gkpre"][1] + 4)
            st.mark(act.activation(gtmp[:], bsum[:], ACT.Abs))
            st.settle()
            st.mark(act.activation(gtmp[:], gtmp[:], ACT.Exp, scale=-1.0))
            st.settle()
            act.activation(gtmp[:], gtmp[:], ACT.Ln, bias=1.0).then_inc(g_log, 1)
            g0 = AT["gv"][0]
            for n, (dst, f) in enumerate(((gout, ACT.Silu), (vg, ACT.Copy))):
                with act.Fori(0, 2) as i:
                    for t in range(TT):
                        act.wait_ge(pe_groups, i * 8 + g0 + 16 * n + t + 1)
                        act.activation(dst[:, t, ds(i * PW, PW)], ps[t][:, 0:PW], f).then_inc(act_freed, 1)

            act.preload_act_table_set("natural_log_exp_and_others")

            def gla_exps(c, b):
                act.wait_ge(g_x, c + 1)
                act.activation(kx[b][:], kx[b][:], ACT.Exp, scale=1.0 / 16)
                act.activation(qx[b][:, 0:3:2], qx[b][:, 0:3:2], ACT.Exp, scale=1.0 / 16)
                act.activation(qx[b][:, 1], bsum[:, :, ds(c * P, P)], ACT.Exp, scale=1.0 / 16)
                act.activation(decay[b][:], bsum[:, :, ds(c * P + P - 1, 1)].rearrange("p a b -> p (a b)"), ACT.Exp,
                               scale=1.0 / 16).then_inc(g_e, 1)

            def gla_kdt(c):
                act.wait_ge(g_t, c + 1)
                act.activation(kdt[:], ps[2][:, 0:2 * P], ACT.Copy).then_inc(g_kd, 1)

            def gla_turn(c, b, more):
                if more:
                    gla_exps(c + 1, 1 - b)
                act.wait_ge(g_o, c + 1)
                stats([ps[5 + h % 2][:, h // 2 * GDV:(h // 2 + 1) * GDV] for h in range(GH)],
                      lambda j: gsq[:, j * GDV:(j + 1) * GDV], 0, GH, 1.0 / GDV, g_r)
                if more:
                    gla_kdt(c + 1)

            gla_exps(0, 0)
            gla_kdt(0)
            with act.Fori(0, TT - 2, 2) as c:
                st.enter(c, 10, 2)
                gla_turn(c, 0, True)
                gla_turn(c + 1, 1, True)
                st.leave((TT - 2) // 2)
            gla_turn(TT - 2, 0, True)
            gla_turn(TT - 1, 1, False)

            act.wait_ge(g_out, TT)
            act.wait_ge(mem_landed, 16)
            stats([memx[:, n, :] for n in range(2)], lambda j: junk_os[:, j, :], 16, 2, 1.0 / D, rstd_ready)
            g0 = AT["qks"][0]
            for n, (dst, sc) in enumerate(((qs, 64 ** -0.5), (ks, 1.0))):
                for j in range(8):
                    act.wait_ge(pe_groups, g0 + 8 * n + j + 1)
                    act.activation(dst[:, j // 2, (j % 2) * HALF:(j % 2 + 1) * HALF], ps[j], ACT.Copy,
                                   scale=sc).then_inc(act_freed, 1)
            g0 = AT["vs"][0]
            with act.Fori(0, 2) as i:
                for t in range(TT):
                    act.wait_ge(pe_groups, i * 8 + g0 + t + 1)
                    act.activation(vs[:, t, ds(i * PW, PW)], ps[t][:, 0:PW], ACT.Copy).then_inc(act_freed, 1)

            def high_part(sp, n):
                key, a, b = unit(n)
                sp.wait(act, st_arg, n - 4)
                sp.wait(act, st_sp, n)
                act.activation(sphi[n % 4][:, 0:b - a], el_of(n), ACT.Identity).then_inc(st_hi, 1)

            def weights(sp, n):
                key, a, b = unit(n)
                sp.wait(act, st_av, n - 4)
                sp.wait(act, st_arg, n)
                act.activation(att[n % 4][:, 0:b - a], scores_of(n), ACT.Exp).then_inc(st_att, 1)

            def head_view(sp, n, r):
                return os_[:, ds(sp.pair(n), 1), :, 64 * r:64 * r + 64].rearrange("p a t d -> p (a t) d")

            def head_squares(sp, n, r):
                sp.wait(act, st_av, n)
                act.activation(head_view(sp, n, r), ps[6 + r].rearrange("p (t d) -> p t d", d=64), ACT.Square).then_inc(st_sq, 1)

            def head_rstd(heads):
                act.wait_ge(st_ss, heads)
                inverse_root(8, 8, 1.0 / 64, st_r)

            def stick_step(sp, k):
                if sp.has(k - 5):
                    weights(sp, k - 5)
                if sp.has(k):
                    sp.wait(act, st_a, k)
                    st.mark(act.activation(el_of(k), el_of(k), ACT.Exp))
                if sp.has(k - 2):
                    high_part(sp, k - 2)
                if sp.has(k):
                    st.settle()
                    act.activation(el_of(k), el_of(k), ACT.Ln, bias=1.0).then_inc(st_l, 1)
                r = 0 if k >= HU else 1
                if k % HU == 6 and sp.has(k - 7):
                    head_squares(sp, k - 7, r)
                if k % HU == 8 and sp.has(k - 9):
                    head_rstd(sp.i * 2 + 1 - r)

            stick(act, stick_step, st, 2 * HU + 2)

            prep("mix", 0, k_col=lambda k: WC_GLA if k < 4 else WC_SB)

            prep("mem", WC_MEM, dst=mhi, cols=MEM, halves=1)

            def high(n, i=None):
                p = MKV_W + n
                landed = 16 * (p // 2 + 1)
                act.wait_ge(raw_landed[p % 2], landed if i is None else i * 16 + landed)
                act.activation(whi[p % 2][:], raw[p % 2][:], ACT.Identity).then_inc(w_hi, 1)

            for n in range(2):
                act.wait_ge(pe_groups, PANEL_END[MKV_W + n - 2])
                high(n)
            act.wait_ge(dve_freed, AT["wout"][2] + 32)
            for hf in range(2):
                token_stats(hf, junk_h)
            g0 = AT["memkv"][0]
            for n, dst in enumerate((kraw, vmem)):
                with act.Fori(0, 2) as i:
                    for j in range(4):
                        act.wait_ge(pe_groups, i * 4 + g0 + 8 * n + j + 1)
                        act.activation(dst[:, j % 2, ds(i * 2 * PW + (j // 2) * PW, PW)], ps[j][:, 0:PW],
                                       ACT.Copy).then_inc(act_freed, 1)
                        if j % 2:
                            high(4 * n + j // 2 + 2, i)
                if n == 0:
                    act.wait_ge(act_freed, AT["memkv"][1] + 8)
                    stats([kraw[:, n2, h * PW:(h + 1) * PW] for n2 in range(2) for h in range(4)],
                          lambda j: ksq[:, j, :], 8, 8, 1.0 / 256, rstd_ready)
            for q in range(4):
                act.wait_ge(pe_groups, AT["kt"][0] + q + 1)
                for k in range(2):
                    ins = act.activation(khat[:, 2 * q + k, :], ps[q][:, k * MEM:(k + 1) * MEM], ACT.Identity,
                                         scale=kcomb[:, k:k + 1])
                ins.then_inc(act_freed, 1)

            prep("h2", WC_XA)
            g0 = AT["q"][0]
            with act.Fori(0, 4) as i:
                for j in range(4):
                    act.wait_ge(pe_groups, i * 5 + g0 + j + 1)
                    act.activation(qt[:, ds(i * 2 + j // 2, 1), (j % 2) * HALF:(j % 2 + 1) * HALF], ps[j],
                                   ACT.Copy).then_inc(act_freed, 1)
            act.wait_ge(dve_freed, AT["q"][2] + 4)
            inverse_root(0, 32, 1.0 / 256, rq_ready)
            act.wait_ge(rq_ready, 1)
            def mout(t):
                act.wait_ge(c_o, t + 1)
                for n in range(2):
                    act.activation(hhi[:, 4 * n:4 * n + 4, t * P:(t + 1) * P], ps[6 + n].rearrange("p (k c) -> p k c", k=4),
                                   ACT.Identity).then_inc(hi_ready, 1)

            for t in range(TT):
                act.wait_ge(c_nb, t + 1)
                if t >= 1:
                    act.wait_ge(c_t, t)
                b = 2 * (t % 2)
                for h in range(4):
                    ins = act.activation(prob[:, h, :], ps[b + h // 2][:, (h % 2) * MEM:(h % 2 + 1) * MEM], ACT.Exp,
                                         bias=mxs[:, 4 + h:5 + h], scale=rstd[:, h * 8 + t:h * 8 + t + 1],
                                         accum_out=mxs[:, 8 + h:9 + h])
                ins.then_inc(c_e, 1)
                if t >= 1:
                    mout(t - 1)
                act.wait_ge(c_t, t + 1)
                act.activation(probt[:], ps_all[:, 4:6, :].rearrange("p b c -> p (b c)"), ACT.Copy).then_inc(c_pt, 1)
            mout(TT - 1)

            for hf in range(2):
                act.wait_ge(dve_freed, AT["h3"][2] - 4 + 4 * hf)
                token_stats(hf, junk_m)
            prep("h3", WC_FFN)

            def gates(first):
                for g in range(4):
                    act.wait_ge(pe_groups, first + g + 1)
                    act.activation(fgate[:, g, :], ps[g], ACT.Silu).then_inc(act_freed, 1)

            def hidden_hi(first):
                for g in range(4):
                    act.wait_ge(f_hid, first + g + 1)
                    act.activation(fhi[:, g // 2, (g % 2) * HALF:(g % 2 + 1) * HALF], fhid[:, g, :], ACT.Copy).then_inc(f_hi, 1)

            gates(FFN_G)
            hidden_hi(0)
            with act.Fori(0, NCH - 1) as i:
                act.wait_ge(f_hid, i * 4 + 4)
                gates(i * 24 + FFN_G + 8)
                hidden_hi(i * 4 + 4)

        @block.vector
        def _(dve):
            st = Steps(dve, dve_step)

            def prep(name, col, hi0, hi=hhi, lo=hlo, cols=HALF, halves=2, k_col=None):
                for hf in range(halves):
                    for k in range(KT):
                        g = hf * KT + k
                        dve.wait_ge(hi_ready, hi0 + g + 1)
                        wc = k_col(k) if k_col else col + k
                        c = slice(hf * cols, (hf + 1) * cols)
                        dve.scalar_tensor_tensor(out=lo[:, k, c], in0=ps[g % 8][:, 0:cols], scalar=wcols[:, wc:wc + 1],
                                                 in1=hi[:, k, c].bitcast(F32), op0=ALU.mult,
                                                 op1=ALU.subtract).then_inc(dve_freed, 1)

            def diagonals(ready0):
                for hf in range(2):
                    dve.wait_ge(rstd_ready, ready0 + hf + 1)
                    for t in range(4 * hf, 4 * hf + 4):
                        ins = dve.tensor_scalar(diag[:, t, :], ident[:], rstd[:, t:t + 1], None, ALU.mult)
                    ins.then_inc(diag_ready, 1)

            def add_panels(name):
                g0 = AT[name][0]
                with dve.Fori(0, 4) as i:
                    for t in range(TT):
                        dve.wait_ge(pe_groups, i * 8 + g0 + t + 1)
                        acc = xres[:, t, ds(i * PW, PW)]
                        dve.tensor_tensor(acc, ps[t][:, 0:PW], acc, ALU.add).then_inc(dve_freed, 1)

            dve.wait_ge(consts_ready, 1)
            diagonals(0)
            dve.wait_ge(wcols_ready, 1)
            prep("h1", WC_MIX, 0)

            dve.memset(state[:], 0.0).then_inc(g_s, 1)
            dve.wait_ge(g_log, 1)
            for pr in range(2):
                st.mark(dve.scalar_tensor_tensor(out=gtmp[:, pr, :], in0=bsum[:, pr, :], scalar=0.0, in1=gtmp[:, pr, :],
                                                 op0=ALU.min, op1=ALU.subtract))
            st.settle()
            for pr in range(2):
                for c in range(TT):
                    cc = slice(c * P, (c + 1) * P)
                    st.mark(dve.tensor_tensor_scan(out=bsum[:, pr, cc], data0=gtmp[:, pr, cc], data1=gtmp[:, pr, cc],
                                                   initial=0.0, op0=ALU.add, op1=ALU.bypass))
            st.settle()

            dve.wait_ge(consts_ready, 1)

            def gla_exponents(c, b):
                bt = bsum[:, :, ds(c * P, P)]
                ref = bsum[:, :, ds(c * P + SBK // 2 - 1, P - SBK // 2 + 1)][:, :, 0:P - SBK + 1:SBK]
                last = bsum[:, :, ds(c * P + P - 1, 1)]
                st.mark(dve.tensor_tensor(kx[b][:], ref.unsqueeze(3).to_broadcast([P, 2, NSB, P]),
                                          bt.unsqueeze(2).to_broadcast([P, 2, NSB, P]), ALU.subtract))
                st.mark(dve.tensor_tensor(qx[b][:, 0].rearrange("p a (s j) -> p a s j", j=SBK),
                                          bt.rearrange("p a (s j) -> p a s j", j=SBK),
                                          ref.unsqueeze(3).to_broadcast([P, 2, NSB, SBK]), ALU.subtract))
                st.mark(dve.tensor_tensor(qx[b][:, 2], last.to_broadcast([P, 2, P]), bt, ALU.subtract))
                st.settle()
                dve.tensor_scalar(kx[b][:], kx[b][:], GCLAMP, None, ALU.min)
                dve.tensor_scalar(qx[b][:, 0], qx[b][:, 0], GCLAMP, None, ALU.min).then_inc(g_x, 1)

            def gla_decayed(c, b):
                dve.wait_ge(g_e, c + 1)
                kc, qc = kg[:, :, ds(c * P, P)], qg[:, :, ds(c * P, P)]
                dve.tensor_tensor(kx[b][:], kx[b][:], kc.unsqueeze(2).to_broadcast([P, 2, NSB, P]), ALU.mult)
                dve.tensor_tensor(qx[b][:, 0:2], qx[b][:, 0:2], qc.unsqueeze(1).to_broadcast([P, 2, 2, P]), ALU.mult)
                dve.tensor_tensor(qx[b][:, 2], qx[b][:, 2], kc, ALU.mult).then_inc(g_m, 1)

            def gla_turn(c, b, more):
                if more:
                    gla_exponents(c + 1, 1 - b)
                dve.wait_ge(g_a, c + 1)
                for r in range(2):
                    ins = dve.tensor_tensor(at_sb[:, r], ps[r][:, 0:2 * P].rearrange("p (a i) -> p a i", a=2),
                                            gmask[:].unsqueeze(1).to_broadcast([P, 2, P]), ALU.mult)
                ins.then_inc(g_at, 1)
                if more:
                    gla_decayed(c + 1, 1 - b)
                dve.wait_ge(g_kv, c + 1)
                for pr in range(2):
                    for r in range(2):
                        rows = slice(64 * r, 64 * r + 64)
                        ins = dve.scalar_tensor_tensor(out=state[rows, pr, :], in0=state[rows, pr, :],
                                                       scalar=decay[b][rows, pr:pr + 1],
                                                       in1=ps[3 + pr][rows, r * GDV:(r + 1) * GDV],
                                                       op0=ALU.mult, op1=ALU.add)
                ins.then_inc(g_s, 1)
                dve.wait_ge(g_r, c + 1)
                for h in range(GH):
                    g = gout[:, ds(c, 1), h * GDV:(h + 1) * GDV]
                    ins = dve.scalar_tensor_tensor(out=g, in0=ps[5 + h % 2][:, h // 2 * GDV:(h // 2 + 1) * GDV].unsqueeze(1),
                                                   scalar=rstd[:, h:h + 1], in1=g, op0=ALU.mult, op1=ALU.mult)
                ins.then_inc(g_out, 1)

            gla_exponents(0, 0)
            gla_decayed(0, 0)
            with dve.Fori(0, TT - 2, 2) as c:
                st.enter(c, 6, 2)
                gla_turn(c, 0, True)
                gla_turn(c + 1, 1, True)
                st.leave((TT - 2) // 2)
            gla_turn(TT - 2, 0, True)
            gla_turn(TT - 1, 1, False)

            dve.wait_ge(rstd_ready, 3)
            for n in range(2):
                ins = dve.tensor_scalar(memx[:, n, :], memx[:, n, :], rstd[:, 16 + n:17 + n], None, ALU.mult)
            ins.then_inc(mem_scaled, 1)

            def bounded(sp, n):
                sp.wait(dve, st_z, n)
                dve.tensor_scalar(el_of(n), scores_of(n), LINEAR, None, ALU.min).then_inc(st_a, 1)

            def softplus(sp, n):
                sp.wait(dve, st_l, n)
                dve.tensor_tensor(el_of(n), scores_of(n), el_of(n), ALU.max).then_inc(st_sp, 1)

            def low_part(sp, n):
                key, a, b = unit(n)
                sp.wait(dve, st_arg, n - 4)
                sp.wait(dve, st_hi, n)
                dve.tensor_tensor(splo[n % 4][:, 0:b - a], el_of(n), sphi[n % 4][:, 0:b - a].bitcast(F32),
                                  ALU.subtract).then_inc(st_lo, 1)

            def sum_later(sp, n):
                key, a, b = unit(n)
                c = max(a, (key + 1) * P)
                sp.wait(dve, st_arg, before(n) if c < b else n - 2)
                if a == key * P:
                    ins = dve.tensor_copy(later[key % 2][:, a:a + P], el_of(n)[:, 0:P])
                if c < b:
                    sp.wait_later(dve, before(n))
                    ins = dve.tensor_tensor(later[key % 2][:, c:b], later[(key + 1) % 2][:, c:b],
                                            el_of(n)[:, c - a:b - a], ALU.add)
                ins.then_inc(st_later, 1)

            def head_sums(sp, n, r, heads):
                dve.wait_ge(st_sq, heads)
                squares = os_[:, ds(sp.pair(n), 1), :, 64 * r:64 * r + 64].rearrange("p a t d -> p (a t) d")
                dve.tensor_reduce(ssq[:, 8:16], squares, AX.X, ALU.add).then_inc(st_ss, 1)

            def head_out(sp, n, r, heads):
                dve.wait_ge(st_r, heads)
                dst = os_[:, ds(sp.pair(n), 1), :, 64 * r:64 * r + 64].rearrange("p a t d -> p (a t) d")
                dve.tensor_tensor(dst, ps[6 + r].rearrange("p (t d) -> p t d", d=64),
                                  rstd[:, 8:16].unsqueeze(2).to_broadcast([P, TT, 64]), ALU.mult).then_inc(st_o, 1)

            def stick_step(sp, k):
                if sp.has(k - 2):
                    softplus(sp, k - 2)
                if sp.has(k):
                    bounded(sp, k)
                if sp.has(k - 3):
                    low_part(sp, k - 3)
                    if unit(k - 3)[0] > 0:
                        sum_later(sp, k - 3)
                r = 0 if k >= HU else 1
                heads = sp.i * 2 + 1 - r
                if k % HU == 7 and sp.has(k - 8):
                    head_sums(sp, k - 8, r, heads)
                if k % HU == 9 and sp.has(k - 10):
                    head_out(sp, k - 10, r, heads)

            stick(dve, stick_step)

            hi_n = 16
            hi_n = 16
            prep("mix", 0, hi_n, k_col=lambda k: WC_GLA if k < 4 else WC_SB)
            hi_n += 16
            prep("mem", WC_MEM, hi_n, hi=mhi, lo=mlo, cols=MEM, halves=1)
            hi_n += 8
            dve.wait_ge(xr_landed, 16 * TT)
            add_panels("wout")
            diagonals(3)
            st.mark(dve.tensor_tensor(kcomb[:], wcols[:, WC_MQ:WC_MQ + 2], wcols[:, WC_MK:WC_MK + 2], ALU.mult))
            st.settle()
            st.mark(dve.tensor_scalar(kcomb[:], kcomb[:], 1.0 / 16, None, ALU.mult))
            st.settle()
            dve.wait_ge(rstd_ready, 6)
            for n in range(2):
                for h in range(4):
                    kk = kraw[:, n, h * PW:(h + 1) * PW]
                    ins = dve.tensor_scalar(kk, kk, rstd[:, 8 + 4 * n + h:9 + 4 * n + h], None, ALU.mult)
            ins.then_inc(kn_ready, 1)
            prep("h2", WC_XA, hi_n)
            hi_n += 16
            with dve.Fori(0, 4) as i:
                for j in range(4):
                    dve.wait_ge(act_freed, i * 4 + AT["q"][1] + j + 1)
                    if j == 0:
                        dve.wait_ge(pe_groups, i * 5 + AT["q"][0])
                    qq = qt[:, ds(i * 2 + j // 2, 1), (j % 2) * HALF:(j % 2 + 1) * HALF]
                    dve.tensor_tensor(qsq[:, j:j + 1, :], qq, qq, ALU.mult).then_inc(q_squared, 1)
                dve.wait_ge(pe_groups, i * 5 + AT["q"][0] + 5)
                dve.tensor_copy(ssq[:, ds(i * 8, 8)], ps[4][:, 0:8]).then_inc(dve_freed, 1)
            dve.wait_ge(rq_ready, 1)
            rq = rstd[:].rearrange("p (h t) -> p h t", t=8)

            def maxima(t):
                dve.wait_ge(c_s, t + 1)
                if t >= 1:
                    dve.wait_ge(c_e, t)
                b = 2 * (t % 2)
                st.mark(dve.tensor_reduce(mxs[:, 0:4], ps_all[:, b:b + 2, :].rearrange("p b (h m) -> p (b h) m", h=2),
                                          AX.X, ALU.max))
                st.settle()
                dve.scalar_tensor_tensor(out=mxs[:, 4:8], in0=mxs[:, 0:4], scalar=-1.0, in1=rq[:, :, t],
                                         op0=ALU.mult, op1=ALU.mult).then_inc(c_nb, 1)

            def mlow(t):
                for n in range(2):
                    dve.wait_ge(hi_ready, hi_n + 2 * t + n + 1)
                    tk = slice(t * P, (t + 1) * P)
                    ins = dve.tensor_tensor(hlo[:, 4 * n:4 * n + 4, tk], ps[6 + n].rearrange("p (k c) -> p k c", k=4),
                                            hhi[:, 4 * n:4 * n + 4, tk].bitcast(F32), ALU.subtract)
                ins.then_inc(c_lo, 1)

            maxima(0)
            for t in range(TT):
                dve.wait_ge(c_e, t + 1)
                st.mark(dve.reciprocal(mxs[:, 12:16], mxs[:, 8:12]))
                st.settle()
                dve.tensor_tensor(prob[:], prob[:], mxs[:, 12:16].unsqueeze(2).to_broadcast([P, 4, MEM]), ALU.mult).then_inc(c_p, 1)
                if t + 1 < TT:
                    maxima(t + 1)
                if t >= 1:
                    mlow(t - 1)
            mlow(TT - 1)
            hi_n += 2 * TT
            add_panels("wmo")
            diagonals(6)
            prep("h3", WC_FFN, hi_n)

            def hidden(first_group, act_first, n_first):
                for g in range(4):
                    dve.wait_ge(pe_groups, first_group + g + 1)
                    dve.wait_ge(act_freed, act_first + g + 1)
                    dve.tensor_tensor(fhid[:, g, :], ps[4 + g], fgate[:, g, :], ALU.mult).then_inc(f_hid, 1)
                for g in range(4):
                    dve.wait_ge(f_hi, n_first + g + 1)
                    c = slice((g % 2) * HALF, (g % 2 + 1) * HALF)
                    dve.tensor_tensor(flo[:, g // 2, c], fhid[:, g, :], fhi[:, g // 2, c].bitcast(F32),
                                      ALU.subtract).then_inc(f_lo, 1)

            def add_down(first_group):
                for g in range(16):
                    t, cc = g // 2, g % 2
                    dve.wait_ge(pe_groups, first_group + g + 1)
                    acc = xres[:, t, cc * HALF:(cc + 1) * HALF]
                    dve.tensor_tensor(acc, ps[(4 + g) % 8], acc, ALU.add).then_inc(dve_freed, 1)

            hidden(FFN_G + 4, FFN_A, 0)
            with dve.Fori(0, NCH - 1) as i:
                add_down(i * 24 + FFN_G + 12)
                hidden(i * 24 + FFN_G + 28, i * 4 + FFN_A + 4, i * 4 + 4)
            add_down(FFN_G + 8 + 24 * (NCH - 1))


_INS = ["x", "mem", "mix_norm_w", "w_in", "w_gk_up", "b_gk", "gla_norm_w", "sb_norm_w", "w_out",
        "xattn_norm_w", "mem_norm_w", "w_mq", "w_mkv", "mq_norm_w", "mk_norm_w", "w_mo",
        "ffn_norm_w", "w_gate_up", "w_down"]


def kernel(**inputs):
    import numpy as np
    import concourse.bacc as bacc
    from concourse.bass_utils import run_bass_kernel_spmd

    nc = bacc.Bacc("TRN2", target_bir_lowering=False, num_devices=1)
    arrays, args = {}, []
    for name in _INS:
        a = np.ascontiguousarray(inputs[name])
        arrays[f"in_{name}"] = a
        args.append(nc.dram_tensor(f"in_{name}", a.shape, mybir.dt.from_np(a.dtype), kind="ExternalInput").ap())
    out = nc.dram_tensor("out_0", (1, SEQ, D), F32, kind="ExternalOutput").ap()
    build(nc, *args, out)
    result = run_bass_kernel_spmd(nc, [arrays], core_ids=[0])
    return result.results[0]["out_0"]
```
